# Optimizing a Trainium2 kernel written in Bass

```python
import math, functools
import jax, jax.numpy as jnp
from jax import lax
import numpy as np

D_MODEL = 1024
BATCH = 1
SEQ = 1024
DEPTH = 1
DEC_BATCH = 8
DEC_SEQ = 1
PAST_LEN = 8192
PAGE_SIZE = 128

MLA_HEADS = 8
MLA_NOPE = 64
MLA_ROPE = 32
MLA_VDIM = 64
Q_LORA = 384
KV_LORA = 256
HG_HEADS = 4
HG_DK = 128
HG_DV = 128
HG_CHUNK = 32
MLA_WIDTH = MLA_HEADS * MLA_VDIM
HG_QK = HG_HEADS * HG_DK
HG_WIDTH = HG_HEADS * HG_DV
MIX_WIDTH = MLA_WIDTH + HG_WIDTH
OFF_CKV = Q_LORA
OFF_KR = OFF_CKV + KV_LORA
OFF_HG = OFF_KR + MLA_ROPE
IN_COLS = OFF_HG + 2 * HG_QK + 2 * HG_WIDTH
MEM_TOKENS = 256
MEM_HEADS = 4
MEM_HDIM = 128
D_FF = 2816
CONV_W = 3

Q_BLOCK = 128
ROPE_BASE = 10000.0
EPS = 1e-6

kernel_name = 'hybrid_mla_hgrn2_decode_step'

def rms_norm(x, g):
    xf = x.astype(jnp.float32)
    y = xf * lax.rsqrt(jnp.mean(xf * xf, axis=-1, keepdims=True) + EPS)
    return (y * g.astype(jnp.float32)).astype(x.dtype)

def rope(x, pos):
    half = x.shape[-1] // 2
    inv = ROPE_BASE ** (-jnp.arange(half, dtype=jnp.float32) / half)
    ang = pos[:, None] * inv[None, :]
    ang = ang.reshape(ang.shape[:1] + (1,) * (x.ndim - 3) + ang.shape[1:])
    cos, sin = jnp.cos(ang), jnp.sin(ang)
    xf = x.astype(jnp.float32)
    x1, x2 = xf[..., :half], xf[..., half:]
    return jnp.concatenate([x1 * cos - x2 * sin, x1 * sin + x2 * cos], axis=-1).astype(x.dtype)

def mla_prompt_attention(q_nope, q_rope, c_kv, k_rope, w_uk, w_uv):
    B, T = c_kv.shape[:2]
    k_nope = jnp.einsum('btl,lhn->bthn', c_kv, w_uk)
    v = jnp.einsum('btl,lhv->bthv', c_kv, w_uv)
    scale = (MLA_NOPE + MLA_ROPE) ** -0.5
    qb = math.gcd(T, Q_BLOCK)
    key_pos = jnp.arange(T)

    def block(i):
        s0 = i * qb
        qn = lax.dynamic_slice_in_dim(q_nope, s0, qb, axis=1)
        qr = lax.dynamic_slice_in_dim(q_rope, s0, qb, axis=1)
        s = (jnp.einsum('bqhn,bkhn->bhqk', qn, k_nope)
             + jnp.einsum('bqhr,bkr->bhqk', qr, k_rope)).astype(jnp.float32) * scale
        q_pos = s0 + jnp.arange(qb)
        s = jnp.where(key_pos[None, :] <= q_pos[:, None], s, -jnp.inf)
        p = jax.nn.softmax(s, axis=-1).astype(v.dtype)
        return jnp.einsum('bhqk,bkhv->bqhv', p, v)

    out = lax.map(block, jnp.arange(T // qb))
    return out.transpose(1, 0, 2, 3, 4).reshape(B, T, MLA_HEADS, MLA_VDIM)

def mla_sample_attention(q_nope, q_rope, c_kv, k_rope, ckv_past, krope_past, w_uk, w_uv):
    T = c_kv.shape[1]
    P = ckv_past.shape[1]
    scale = (MLA_NOPE + MLA_ROPE) ** -0.5
    q_lat = jnp.einsum('bthn,lhn->bthl', q_nope, w_uk)
    s_past = (jnp.einsum('bthl,bpl->bhtp', q_lat, ckv_past)
              + jnp.einsum('bthr,bpr->bhtp', q_rope, krope_past))
    s_new = (jnp.einsum('bthl,bsl->bhts', q_lat, c_kv)
             + jnp.einsum('bthr,bsr->bhts', q_rope, k_rope))
    causal = jnp.tril(jnp.ones((T, T), dtype=bool))
    s_new = jnp.where(causal, s_new.astype(jnp.float32), -jnp.inf)
    s = jnp.concatenate([s_past.astype(jnp.float32), s_new], axis=-1) * scale
    p = jax.nn.softmax(s, axis=-1).astype(c_kv.dtype)
    lat = (jnp.einsum('bhtp,bpl->bthl', p[..., :P], ckv_past)
           + jnp.einsum('bhts,bsl->bthl', p[..., P:], c_kv))
    return jnp.einsum('bthl,lhv->bthv', lat, w_uv)

def hgrn2_scan(q, k, v, log_f, s0):
    B, T, H, DK = q.shape
    DV = v.shape[-1]
    c = math.gcd(T, HG_CHUNK)
    n = T // c

    def to_chunks(a):
        return a.astype(jnp.float32).reshape(B, n, c, H, a.shape[-1]).transpose(1, 0, 3, 2, 4)

    qc, kc, vc, gc = to_chunks(q), to_chunks(k), to_chunks(v), to_chunks(log_f)
    mask = jnp.tril(jnp.ones((c, c), dtype=bool))

    def step(S, inp):
        qi, ki, vi, gi = inp
        b = jnp.cumsum(gi, axis=-2)
        q_t = qi * jnp.exp(b)
        a = jnp.einsum('bhtd,bhsd->bhts', q_t, ki * jnp.exp(-b))
        a = jnp.where(mask, a, 0.0)
        o = jnp.einsum('bhts,bhsv->bhtv', a, vi) + jnp.einsum('bhtd,bhdv->bhtv', q_t, S)
        decay = jnp.exp(b[..., -1, :])
        S = decay[..., None] * S + jnp.einsum('bhsd,bhsv->bhdv', ki * jnp.exp(b[..., -1:, :] - b), vi)
        return S, o

    S, o = lax.scan(step, s0.astype(jnp.float32), (qc, kc, vc, gc))
    o = o.transpose(1, 0, 3, 2, 4).reshape(B, T, H, DV)
    return o, S

def hgrn2_group(zh, lb, g_norm, s0):
    B, T, _ = zh.shape
    q = zh[..., :HG_QK].reshape(B, T, HG_HEADS, HG_DK)
    f_raw = zh[..., HG_QK:2 * HG_QK].astype(jnp.float32)
    i_in = zh[..., 2 * HG_QK:2 * HG_QK + HG_WIDTH].reshape(B, T, HG_HEADS, HG_DV)
    gate = zh[..., 2 * HG_QK + HG_WIDTH:]
    f = lb + (1.0 - lb) * jax.nn.sigmoid(f_raw)
    k = (1.0 - f).reshape(B, T, HG_HEADS, HG_DK)
    log_f = jnp.log(f).reshape(B, T, HG_HEADS, HG_DK)
    o, S = hgrn2_scan(q, k, i_in, log_f, s0)
    o = rms_norm(o, g_norm).reshape(B, T, HG_WIDTH) * jax.nn.silu(gate.astype(jnp.float32))
    return o.astype(zh.dtype), S

def memory_kv(mem, g_mem, w_mk, w_mv):
    m = rms_norm(mem, g_mem)
    k = jnp.einsum('bmd,dhe->bmhe', m, w_mk)
    v = jnp.einsum('bmd,dhe->bmhe', m, w_mv)
    return k, v

def memory_attention(h, mem_k, mem_v, w_mq, w_mo):
    q = jnp.einsum('btd,dhe->bthe', h, w_mq)
    s = jnp.einsum('bthe,bmhe->bhtm', q, mem_k).astype(jnp.float32) * (MEM_HDIM ** -0.5)
    p = jax.nn.softmax(s, axis=-1).astype(mem_v.dtype)
    o = jnp.einsum('bhtm,bmhe->bthe', p, mem_v)
    return jnp.einsum('bthe,hed->btd', o, w_mo)

def conv_ffn(h, prefix, w_up, conv_w, conv_b, w_down):
    T = h.shape[1]
    ab = jnp.einsum('btd,df->btf', h, w_up)
    a, gate_in = ab[..., :D_FF], ab[..., D_FF:]
    ext = jnp.concatenate([prefix.astype(a.dtype), a], axis=1)
    conv = conv_b
    for tap in range(CONV_W):
        conv = conv + ext[:, tap:tap + T] * conv_w[tap]
    y = jnp.einsum('btf,fd->btd', jax.nn.silu(conv) * gate_in, w_down)
    return y, ext[:, T:]

def trunk_layer(x, start, mla_attend, s0, conv_prefix, mem_k, mem_v, p):
    B, T, _ = x.shape
    pos = jnp.arange(T, dtype=jnp.float32) + start
    h = rms_norm(x, p['norm_mix'])
    z = jnp.einsum('btd,dc->btc', h, p['w_in'])
    c_q = rms_norm(z[..., :OFF_CKV], p['norm_q'])
    c_kv = rms_norm(z[..., OFF_CKV:OFF_KR], p['norm_kv'])
    k_rope = rope(z[..., OFF_KR:OFF_HG], pos)
    q = jnp.einsum('btc,chd->bthd', c_q, p['w_uq'])
    q_nope, q_rope = q[..., :MLA_NOPE], rope(q[..., MLA_NOPE:], pos)
    o_mla = mla_attend(q_nope, q_rope, c_kv, k_rope).reshape(B, T, MLA_WIDTH)
    o_hg, s_new = hgrn2_group(z[..., OFF_HG:], p['lb'], p['norm_hg'], s0)
    x = x + jnp.einsum('btc,cd->btd', jnp.concatenate([o_mla, o_hg], axis=-1), p['w_out'])
    x = x + memory_attention(rms_norm(x, p['norm_memx']), mem_k, mem_v, p['w_mq'], p['w_mo'])
    y, conv_tail = conv_ffn(rms_norm(x, p['norm_ffn']), conv_prefix, p['w_up'], p['conv_w'], p['conv_b'], p['w_down'])
    x = x + y
    return x, c_kv, k_rope, s_new, conv_tail

def setup_inputs(seed: int = 0) -> dict:
    key = jax.random.key(seed)
    ks = iter(jax.random.split(key, 48))

    def nrm(shape, scale):
        return jax.random.normal(next(ks), shape, jnp.float32) * scale

    def gain(shape):
        return 1.0 + 0.01 * jax.random.normal(next(ks), shape, jnp.float32)

    n_pages = PAST_LEN // PAGE_SIZE
    n_used = DEC_BATCH * n_pages
    n_pool = n_used + max(1, n_used // 4)
    page_table = jax.random.permutation(next(ks), n_pool)[:n_used].reshape(DEC_BATCH, n_pages).astype(jnp.int32)
    return {
        'x_prompt': nrm((BATCH, SEQ, D_MODEL), 1.0),
        'x_sample': nrm((DEC_BATCH, DEC_SEQ, D_MODEL), 1.0),
        'mem_prompt': nrm((BATCH, MEM_TOKENS, D_MODEL), 1.0),
        'cache_ckv': nrm((DEPTH, n_pool, PAGE_SIZE, KV_LORA), 1.0),
        'cache_krope': nrm((DEPTH, n_pool, PAGE_SIZE, MLA_ROPE), 1.0),
        'page_table': page_table,
        'cache_mem_k': nrm((DEPTH, DEC_BATCH, MEM_TOKENS, MEM_HEADS, MEM_HDIM), 1.0),
        'cache_mem_v': nrm((DEPTH, DEC_BATCH, MEM_TOKENS, MEM_HEADS, MEM_HDIM), 1.0),
        'state_hgrn': nrm((DEPTH, DEC_BATCH, HG_HEADS, HG_DK, HG_DV), 0.5),
        'state_conv': nrm((DEPTH, DEC_BATCH, CONV_W - 1, D_FF), 1.0),
        'norm_mix': gain((DEPTH, D_MODEL)),
        'w_in': nrm((DEPTH, D_MODEL, IN_COLS), D_MODEL ** -0.5),
        'norm_q': gain((DEPTH, Q_LORA)),
        'norm_kv': gain((DEPTH, KV_LORA)),
        'w_uq': nrm((DEPTH, Q_LORA, MLA_HEADS, MLA_NOPE + MLA_ROPE), Q_LORA ** -0.5),
        'w_uk': nrm((DEPTH, KV_LORA, MLA_HEADS, MLA_NOPE), KV_LORA ** -0.5),
        'w_uv': nrm((DEPTH, KV_LORA, MLA_HEADS, MLA_VDIM), KV_LORA ** -0.5),
        'hg_lb_raw': nrm((DEPTH + 1, HG_QK), 0.1),
        'norm_hg': gain((DEPTH, HG_DV)),
        'w_out': nrm((DEPTH, MIX_WIDTH, D_MODEL), MIX_WIDTH ** -0.5),
        'norm_memx': gain((DEPTH, D_MODEL)),
        'norm_mem': gain((DEPTH, D_MODEL)),
        'w_mq': nrm((DEPTH, D_MODEL, MEM_HEADS, MEM_HDIM), D_MODEL ** -0.5),
        'w_mk': nrm((DEPTH, D_MODEL, MEM_HEADS, MEM_HDIM), D_MODEL ** -0.5),
        'w_mv': nrm((DEPTH, D_MODEL, MEM_HEADS, MEM_HDIM), D_MODEL ** -0.5),
        'w_mo': nrm((DEPTH, MEM_HEADS, MEM_HDIM, D_MODEL), (MEM_HEADS * MEM_HDIM) ** -0.5),
        'norm_ffn': gain((DEPTH, D_MODEL)),
        'w_up': nrm((DEPTH, D_MODEL, 2 * D_FF), D_MODEL ** -0.5),
        'conv_w': nrm((DEPTH, CONV_W, D_FF), CONV_W ** -0.5),
        'conv_b': nrm((DEPTH, D_FF), 0.01),
        'w_down': nrm((DEPTH, D_FF, D_MODEL), D_FF ** -0.5),
        'norm_final': gain((D_MODEL,)),
    }

def reference(x_prompt, x_sample, mem_prompt, cache_ckv, cache_krope, page_table, cache_mem_k, cache_mem_v,
              state_hgrn, state_conv, norm_mix, w_in, norm_q, norm_kv, w_uq, w_uk, w_uv, hg_lb_raw, norm_hg,
              w_out, norm_memx, norm_mem, w_mq, w_mk, w_mv, w_mo, norm_ffn, w_up, conv_w, conv_b, w_down,
              norm_final):
    lb_all = jnp.cumsum(jax.nn.softmax(hg_lb_raw.astype(jnp.float32), axis=0), axis=0)
    past_len = page_table.shape[1] * cache_ckv.shape[2]
    bp, db = x_prompt.shape[0], x_sample.shape[0]
    xp, xs = x_prompt, x_sample
    ckv_p_l, kr_p_l, mk_p_l, mv_p_l, s_p_l, cv_p_l = [], [], [], [], [], []
    ckv_s_l, kr_s_l, s_s_l, cv_s_l = [], [], [], []
    for l in range(DEPTH):
        p = {'norm_mix': norm_mix[l], 'w_in': w_in[l], 'norm_q': norm_q[l], 'norm_kv': norm_kv[l],
             'w_uq': w_uq[l], 'lb': lb_all[l], 'norm_hg': norm_hg[l], 'w_out': w_out[l],
             'norm_memx': norm_memx[l], 'w_mq': w_mq[l], 'w_mo': w_mo[l], 'norm_ffn': norm_ffn[l],
             'w_up': w_up[l], 'conv_w': conv_w[l], 'conv_b': conv_b[l], 'w_down': w_down[l]}
        mk_p, mv_p = memory_kv(mem_prompt, norm_mem[l], w_mk[l], w_mv[l])
        attend_p = functools.partial(mla_prompt_attention, w_uk=w_uk[l], w_uv=w_uv[l])
        s0_p = jnp.zeros((bp, HG_HEADS, HG_DK, HG_DV), jnp.float32)
        pre_p = jnp.zeros((bp, CONV_W - 1, D_FF), x_prompt.dtype)
        xp, ckv_p, kr_p, s_p, cv_p = trunk_layer(xp, 0, attend_p, s0_p, pre_p, mk_p, mv_p, p)
        ckv_past = cache_ckv[l, page_table].reshape(db, past_len, KV_LORA)
        kr_past = cache_krope[l, page_table].reshape(db, past_len, MLA_ROPE)
        attend_s = functools.partial(mla_sample_attention, ckv_past=ckv_past, krope_past=kr_past,
                                     w_uk=w_uk[l], w_uv=w_uv[l])
        xs, ckv_s, kr_s, s_s, cv_s = trunk_layer(xs, past_len, attend_s, state_hgrn[l], state_conv[l],
                                                 cache_mem_k[l], cache_mem_v[l], p)
        ckv_p_l.append(ckv_p)
        kr_p_l.append(kr_p)
        mk_p_l.append(mk_p)
        mv_p_l.append(mv_p)
        s_p_l.append(s_p.astype(x_prompt.dtype))
        cv_p_l.append(cv_p)
        ckv_s_l.append(ckv_s)
        kr_s_l.append(kr_s)
        s_s_l.append(s_s.astype(state_hgrn.dtype))
        cv_s_l.append(cv_s.astype(state_conv.dtype))
    y_prompt = rms_norm(xp, norm_final)
    y_sample = rms_norm(xs, norm_final)
    return (y_prompt, y_sample,
            jnp.stack(ckv_p_l), jnp.stack(kr_p_l), jnp.stack(mk_p_l), jnp.stack(mv_p_l),
            jnp.stack(s_p_l), jnp.stack(cv_p_l),
            jnp.stack(ckv_s_l), jnp.stack(kr_s_l), jnp.stack(s_s_l), jnp.stack(cv_s_l))


_drawn_inputs = setup_inputs


def setup_inputs(seed=0):
    import zlib

    import numpy as np

    out = dict(_drawn_inputs(seed))
    spreads = {}
    factors = {'cache_ckv': 4.517,
     'cache_krope': 8.0,
     'norm_mix': 5.396,
     'norm_q': 8.0,
     'norm_kv': 15.488,
     'norm_hg': 23.032,
     'norm_memx': 25.217,
     'norm_mem': 17.327,
     'norm_ffn': 31.348,
     'conv_b': 38.427,
     'norm_final': 33.59}
    for name, (base, spread) in spreads.items():
        noise = np.random.default_rng([zlib.crc32(name.encode()), seed]).standard_normal(out[name].shape)
        drawn = base * np.exp(spread * noise) if base else spread * noise
        out[name] = __import__('jax').numpy.asarray(drawn.astype(out[name].dtype))
    for name, factor in factors.items():
        out[name] = (out[name] * factor).astype(out[name].dtype)
    return out
```

```python
from contextlib import ExitStack

import numpy as np

import concourse.bass as bass
from concourse import mybir

ALU = mybir.AluOpType
ACT = mybir.ActivationFunctionType
AX = mybir.AxisListType.X
F32 = mybir.dt.float32
F32R = mybir.dt.float32r
I32 = mybir.dt.int32
U32 = mybir.dt.uint32

P = 128
D = 1024
KD = D // P
T = 1024
NT = T // P
NS = 8
TT = T + NS
NCH = 3
CH = TT // NCH
PAGE = 128
NPG = 64
H = 8
NOPE, ROPE, VD = 64, 32, 64
QK = NOPE + ROPE
QL, KVL = 384, 256
KQ, KV = QL // P, KVL // P
HG = 4
DK = 128
CK = 32
IN_COLS = 2720
OFF_CKV = QL
OFF_KR = OFF_CKV + KVL
OFF_HG = OFF_KR + ROPE
MT = 256
MH = 4
ME = MH * P
FF = 2816
NF = FF // P
CW = 3
EPS = 1e-6
XMIN = -87.0
SCALE = float(QK) ** -0.5
MSCALE = float(P) ** -0.5
NEG = -1e30
GP = 16
NG = NPG // GP
GT = NS * NG
FPARTS = [range(0, 5), range(5, 10), range(10, 14), range(14, 18), range(18, 22)]
FSLOTS = 6


def build_program(nc, i, o):
    ctx = ExitStack()
    with ctx:
        top = [(nc.sbuf_base + 31) // 32 * 32]

        def at(name, shape, dt, off):
            return nc.alloc_sbuf_tensor_at(name, shape, dt, offset=off)

        def size(shape):
            return int(np.prod(shape[1:])) * 4

        def keep(name, shape, dt=F32):
            off = top[0]
            top[0] += (size(shape) + 31) // 32 * 32
            return at(name, shape, dt, off)

        def place(start, end, *items):
            out = []
            for name, shape, dt in items:
                out.append(at(name, shape, dt, start))
                start += (size(shape) + 31) // 32 * 32
            assert start <= end, (items[-1][0], start - end)
            return out

        ident = keep("ident", [P, P])
        causal = keep("causal", [P, P])
        hmask = keep("hmask", [P, P], U32)
        ones = keep("ones", [P, P])
        sel = keep("sel", [P, 8])
        rowof = keep("rowof", [P, 1])
        selv = keep("selv", [P, 2, MH, 4])
        eps = keep("eps", [P, 1])
        gains = keep("gains", [P, 56])
        convc = keep("convc", [P, 88])
        atail = keep("atail", [P, NF, 10])
        sconv = keep("sconv", [P, NF, 16])
        lbt = keep("lbt", [P, 24])
        small = keep("small", [P, 128])
        idx = keep("idx", [P, GT], I32)
        XT = keep("XT", [P, KD, TT])
        wraw = [keep(f"wraw{n}", [P, 8 * P]) for n in range(2)]
        whi = [keep(f"whi{n}", [P, 8 * P], F32R) for n in range(2)]
        wlo = [keep(f"wlo{n}", [P, 8 * P], F32R) for n in range(2)]
        S0 = top[0]
        RB1 = keep("RB1", [P, TT])
        RB2 = keep("RB2", [P, TT])
        SQ = keep("SQ", [P, TT])
        SS = keep("SS", [P, TT])
        S1 = top[0]
        A0 = top[0]
        XH = keep("XH", [P, KD, TT], F32R)
        XL = keep("XL", [P, KD, TT], F32R)
        A1 = B0 = top[0]
        B1 = 229344
        PS = ctx.enter_context(nc.psum_tensor("PS", [P, 8, 512], F32))

        xstage = place(B0, B1, *[(f"xstage{n}", [P, D], F32) for n in range(4)])
        crow, cvrow, scrow = place(B0 + 4 * 4096, B1, ("crow", [54, P], F32), ("cvrow", [88, P], F32), ("scrow", [16, FF], F32))
        (HGO, t0, t1, t2, tqa, v0, vtok, ketok, v4, Sst, AT, RM, dec, smp) = place(
            B0, B1, ("HGO", [P, HG, TT], F32), *[(n, [P, TT], F32) for n in ("t0", "t1", "t2", "tqa", "v0")],
            ("vtok", [P, NT, P], F32), ("ketok", [P, NT, P], F32), ("v4", [P, 4, 4, P], F32),
            ("Sst", [P, 17, P], F32), ("AT", [P, 4, P], F32), ("RM", [P, 256], F32), ("dec", [P, 32], F32), ("smp", [P, 64], F32))
        tq = [tqa, SQ]
        SB = at("SB", [P, NS, P], F32, S0 + 4128)
        ON = AT
        OTMP = at("OTMP", [P, NS, P], F32, S0 + 3 * 4128)
        (ckvT, trig, cqr, cqh, cql) = place(
            B0 + HG * TT * 4, B1, ("ckvT", [P, KV, TT], F32), ("trig", [P, TT], F32),
            ("cqr", [P, KQ, TT], F32), ("cqh", [P, KQ, TT], F32R), ("cql", [P, KQ, TT], F32R))
        R1 = B0 + HG * TT * 4
        Q0 = R1 + KV * TT * 4 + TT * 4
        V, ckh, ckl = place(Q0, B1, ("V", [P, NT, 512], F32), ("ckh", [P, KV, TT], F32R),
                               ("ckl", [P, KV, TT], F32R))
        ckvo, kro = place(Q0 + 16384, B1, ("ckvo", [P, NT + 1, KVL], F32), ("kro", [P, NT + 1, ROPE], F32))
        MO, PT1 = place(Q0 + 16384, B1, ("MO", [P, 4, TT], F32), ("PT1", [P, NT, P], F32))
        Pr = place(R1, Q0, *[(f"Pr{n}", [P, T], F32) for n in range(2)])
        PT0, = place(R1 + KV * TT * 4, Q0, ("PT0", [P, NT, P], F32))
        PTr = [PT0, PT1]
        qT, kT = place(A0, A1, ("qT", [P, H, TT], F32), ("kT", [P, H, TT], F32))
        wuv = at("wuv", [P, KV, 512], F32, S0 + 3 * 4128)
        wuk = at("wuk", [P, KV, 512], F32, S0 + 2 * 4128)
        ring = place(A0, A1, *[x for n in range(3) for x in ((f"rc{n}", [P, GP, KVL], F32), (f"rk{n}", [P, GP, ROPE], F32))],
                     ("Oacc", [P, NS, KVL], F32), ("qlat", [P, KV, NS, 32], F32))
        rc, rk, Oacc, qlat = ring[0:6:2], ring[1:6:2], ring[6], ring[7]
        KT, KRT, qrz, Og, PTs = place(R1, Q0 + 16384, ("KT", [P, 4, KV, 512], F32), ("KRT", [P, 4, P], F32),
                                      ("qrz", [P, NS, 4, 32], F32), ("Og", [P, NG, KVL], F32), ("PTs", [P, 4, P], F32))
        wukT = at("wukT", [P, H, KVL], F32, R1)
        Ps = place(S0, S0 + 4128, *[(f"Ps{n}", [P, 512], F32) for n in range(2)])
        dsm = at("dsm", [P, TT], F32, S0 + 4128)
        nmax, lsum, nmS, Lseq, wgt, fac = (dsm[:, a:b] for a, b in ((0, 32), (32, 64), (64, 72), (72, 80), (80, 84), (88, 96)))
        lprod = dsm[:, 96:100]
        nMx, snew, wnew, expd = dsm[0:NS, 104:136], dsm[0:NS, 136:168], dsm[0:NS, 168:200], dsm[0:NS, 200:328]
        sprod = dsm[0:NS, 328:584].rearrange("p (b h) -> p b h", b=NS)
        LS, WD = dsm[:, 584:648], dsm[0:NS, 648:712]
        lat = dsm[:, 712:840].rearrange("p (c b h) -> p c b h", c=KV, b=NS)
        ltmp = dsm[:, 840:968].rearrange("p (c b h) -> p c b h", c=KV, b=NS)
        krs0 = dsm[0:ROPE, 968:976]
        CHi, CLo = place(A0, A1, ("CHi", [P, KD, TT], F32R), ("CLo", [P, KD, TT], F32R))
        BH, BL = place(B0, B1, ("BH", [P, KD, TT], F32R), ("BL", [P, KD, TT], F32R))
        qm, MKT, MV = place(A0, A1, ("qm", [P, MH, TT], F32), ("MKT", [P, MH, MT], F32), ("MV", [P, 2, ME], F32))
        M0 = A0 + MH * TT * 4 + 8192
        mraw0, mraw1, memT, mh, ml, mvT = place(M0, A1, ("mraw0", [P, D], F32), ("mraw1", [P, D], F32), ("memT", [P, KD, MT], F32),
                                                ("mh", [P, KD, MT], F32R), ("ml", [P, KD, MT], F32R), ("mvT", [P, MH, MT], F32))
        mraw = [mraw0, mraw1]
        omh, oml, Pm0, Pm1, = place(M0, A1, ("omh", [P, MH, TT], F32R), ("oml", [P, MH, TT], F32R),
                                    ("Pm0", [P, 2, MT], F32), ("Pm1", [P, 2, MT], F32))
        Pm = [Pm0, Pm1]
        mko, PTm0, PTm1, QS, OH, prod, sc, scr, pm, sK0, sK1, *sV = place(
            B0, B1, ("mko", [P, 2, ME], F32), ("PTm0", [P, 4, P], F32), ("PTm1", [P, 4, P], F32), ("QS", [NS, ME], F32),
            ("OH", [NS, NS, P], F32), ("prod", [P, 2, ME], F32), ("sc", [P, 2, 32], F32), ("scr", [P, MT], F32),
            ("pm", [P, 2, 32], F32), ("sK0", [P, 2, ME], F32), ("sK1", [P, 2, ME], F32),
            *[(f"sV{n}", [P, 2, ME], F32) for n in range(NS)])
        PTm, sK = [PTm0, PTm1], [sK0, sK1]
        acth, actl, ab, ct, cu = place(A0, A1, ("acth", [P, FSLOTS, TT], F32R), ("actl", [P, FSLOTS, TT], F32R),
                                       ("ab", [P, TT + 2], F32), ("ct", [P, TT], F32), ("cu", [P, TT], F32))
        XG, *yst = place(B0, B1, ("XG", [P, KD, TT], F32), *[(f"yst{n}", [P, D], F32) for n in range(4)])
        cvs, = place(B0 + KD * TT * 4, B1, ("cvs", [10, FF], F32))

        def rows_of(h):
            return smp[:, 24 + 16 * (h % 2):40 + 16 * (h % 2)]

        def sem(name):
            return ctx.enter_context(nc.semaphore(name))

        psum_full = sem("psum_full")
        freed = {"v": sem("freed_v"), "s": sem("freed_s")}
        ident_in, consts_in = sem("ident_in"), sem("consts_in")
        x_in = [sem(f"x_in{n}") for n in range(4)]
        w_in_sem = [sem(f"w_in{n}") for n in range(2)]
        w_hi_done, w_split = sem("w_hi_done"), sem("w_split")
        hi_done, lo_done, sq_done, ss_done = sem("hi_done"), sem("lo_done"), sem("sq_done"), sem("ss_done")
        rstd_new = sem("rstd_new")
        vstep, sstep, pstep = sem("vstep"), sem("sstep"), sem("pstep")
        pg_new = sem("pg_new")
        sb_in, sb_out, hst_out = sem("sb_in"), sem("sb_out"), sem("hst_out")
        lb_diff, lb_exp = sem("lb_diff"), sem("lb_exp")
        f_raw, g_raw = sem("f_raw"), sem("g_raw")
        f_exp, f_new, f_log, b_new, b_exp, b_nexp = [sem(n) for n in ("f_exp", "f_new", "f_log", "b_new", "b_exp", "b_nexp")]
        gate_new, g_exp, qk_new, v4_new = sem("gate_new"), sem("g_exp"), sem("qk_new"), sem("v4_new")
        o_sq, o_ms, o_rstd = sem("o_sq"), sem("o_ms"), sem("o_rstd")
        os_ms, os_rstd, os_new = sem("os_ms"), sem("os_rstd"), sem("os_new")
        ones_set = sem("ones_set")
        wuk_in, lat_zero, qs_new, qz_new = sem("wuk_in"), sem("lat_zero"), sem("qs_new"), sem("qz_new")
        page_in = [sem(f"page_in{n}") for n in range(3)]
        g_max, seq_w, seq_wd, seq_o = sem("g_max"), sem("seq_w"), sem("seq_wd"), sem("seq_o")
        c_new, c_exp, c_diff, c_fac, ls_new, lat_new = [sem(n) for n in ("c_new", "c_exp", "c_diff", "c_fac", "ls_new", "lat_new")]
        cat_hi, cat_lo = sem("cat_hi"), sem("cat_lo")
        mem_in, mk_out, mv_out = sem("mem_in"), sem("mk_out"), sem("mv_out")
        m_max, m_new, om_hi = sem("m_max"), sem("m_new"), sem("om_hi")
        sk_in, sv_in = [sem(f"sk_in{n}") for n in range(2)], sem("sv_in")
        qs_set, prod_done, s_max, s_exp, s_new2 = sem("qs_set"), sem("prod_done"), sem("s_max"), sem("s_exp"), sem("s_new2")
        ab_new, conv_new, conv_exp, act_new, act_hi, act_lo = [sem(n) for n in ("ab_new", "conv_new", "conv_exp", "act_new", "act_hi", "act_lo")]
        tail_out = sem("tail_out")
        y_out = [sem(f"y_out{n}") for n in range(4)]
        cs_out = sem("cs_out")
        trig_in, wuv_in, ckv_out, kr_out = sem("trig_in"), sem("wuv_in"), sem("ckv_out"), sem("kr_out")
        kv_sq, kv_sum, kv_new, kv_hi, kv_lo, krT_new = [sem(n) for n in ("kv_sq", "kv_sum", "kv_new", "kv_hi", "kv_lo", "krT_new")]
        trigq_new, q_new, krk_new = sem("trigq_new"), sem("q_new"), sem("krk_new")
        even_done = sem("even_done")
        p_max, p_new = sem("p_max"), sem("p_new")

        uses, nth, last_of = {}, {"v": 0, "s": 0}, {}

        def use(key, banks, by):
            before = [last_of[b] for b in banks if b in last_of]
            nth[by] += 1
            uses[key] = (len(uses) + 1, banks, by, nth[by], before)
            for b in banks:
                last_of[b] = (by, nth[by])

        dense_set = [0]

        def use_dense(key, by="v"):
            dense_set[0] ^= 1
            use(key, [3 * dense_set[0] + n for n in range(3)], by)

        def use_sums(key):
            use(key, [3 * (dense_set[0] ^ 1) + n for n in range(3)], "s")

        def full(eng, key):
            eng.wait_ge(psum_full, uses[key][0])

        def emptied(eng, key):
            eng.wait_ge(freed[uses[key][2]], uses[key][3])

        def bank(key, n=0):
            return PS[:, uses[key][1][n], :]

        def chunks(key, lo=0, hi=P, n=CH):
            b = uses[key][1]
            return PS[lo:hi, b[0]:b[0] + NCH, 0:n]

        def by3(ap):
            return ap.rearrange("p (c n) -> p c n", c=NCH)

        jobs, job_no = [], {}

        def job(name, k, pieces):
            job_no[name] = len(jobs)
            jobs.append((name, k, pieces))

        def cols(w, a, b):
            return w[:, a:b].rearrange("(k p) m -> p k m", p=P)

        w_in, w_uq = i["w_in"][0], i["w_uq"][0].rearrange("c h d -> c (h d)")
        w_uk, w_uv = i["w_uk"][0].rearrange("l h n -> l (h n)"), i["w_uv"][0].rearrange("l h n -> l (h n)")
        for h in range(HG):
            for n, name in enumerate(("f", "g", "q", "i")):
                base = OFF_HG + {"q": 0, "f": 512, "i": 1024, "g": 1536}[name] + h * P
                job((name, h), KD, [(0, cols(w_in, base, base + P))])
        for c in range(KV):
            job(("ckv", c), KD, [(0, cols(w_in, OFF_CKV + c * P, OFF_CKV + (c + 1) * P))])
        job("kr", KD, [(0, cols(w_in, OFF_KR - NOPE, OFF_KR + ROPE)), (96, cols(w_in, OFF_KR + 16, OFF_KR + 32)),
                       (112, cols(w_in, OFF_KR, OFF_KR + 16))])
        for c in range(KQ):
            job(("cq", c), KD, [(0, cols(w_in, c * P, (c + 1) * P))])
        for h in range(H):
            job(("uq", h), KQ, [(0, cols(w_uq, h * QK, h * QK + QK)), (96, cols(w_uq, h * QK + 80, h * QK + 96)),
                                (112, cols(w_uq, h * QK + 64, h * QK + 80))])
        for p2 in range(H // 2):
            job(("uk", p2), KV, [(0, cols(w_uk, p2 * P, p2 * P + P))])

        w_out, w_mo = i["w_out"][0], i["w_mo"][0].rearrange("h e d -> (h e) d")
        w_mq, w_mk, w_mv = (i[n][0].rearrange("d h e -> d (h e)") for n in ("w_mq", "w_mk", "w_mv"))
        w_up, w_down = i["w_up"][0], i["w_down"][0]
        for c in range(KD):
            job(("out", c), KD, [(0, cols(w_out, c * P, c * P + P))])
        for name, w in (("mq", w_mq), ("mk", w_mk), ("mv", w_mv)):
            for h in range(MH):
                job((name, h), KD, [(0, cols(w, h * P, h * P + P))])
        for c in range(KD):
            job(("mo", c), MH, [(0, cols(w_mo, c * P, c * P + P))])

        def ffn_order():
            for n, part in enumerate(FPARTS):
                for f in part:
                    if n == 0 or f != part[0]:
                        yield "up", f
                if n + 1 < len(FPARTS):
                    yield "up", FPARTS[n + 1][0]
                for c in range(KD):
                    yield "down", (n, c)

        for kind, what in ffn_order():
            if kind == "up":
                job(("a", what), KD, [(0, cols(w_up, what * P, what * P + P))])
                job(("b", what), KD, [(0, cols(w_up, FF + what * P, FF + what * P + P))])
            else:
                n, c = what
                f0, f1 = FPARTS[n][0], FPARTS[n][-1] + 1
                job(("down", n, c), f1 - f0, [(0, cols(w_down[f0 * P:f1 * P], c * P, c * P + P))])

        def wtile(ring, j):
            k = jobs[j][1]
            return ring[j % 2][:, 0:k * P].rearrange("p (k m) -> p k m", k=k)

        hi_before, ss_before, a_, b_ = {}, {}, 0, 0
        for name, n in (("mix", KD), ("q", KQ), ("memx", KD), ("mem", KD), ("ffn", KD), ("final", KD)):
            hi_before[name], ss_before[name] = a_, b_
            a_, b_ = a_ + n, b_ + n - 1

        for n in range(NT + 1):
            if n == 4:
                use("cst", [2], "v")
                use("scv", [3], "v")
                use("idx", [4], "v")
            for half in range(2):
                use(("x", n, half), [(2 * n + half) % 8], "sv"[half])

        def plan_o(h, half):
            use(("o", h, half), [6], "v")
            use(("ot", h, half), [7], "v")

        def plan_u(h, half):
            for n in range(4):
                use(("u", h, half, n), [(4 * half + n) % 6], "v")
            use(("a", h, half), [7], "v")

        def plan_turn(h):
            use(("tv", h, 0), [6], "s")
            use(("tv", h, 1), [7], "s")
            use(("ts", h), [6], "v")

        def plan_turn_keys_of(h):
            for half in range(2):
                use(("tk", h, half), [6 + half], "s")

        def plan_samp(h):
            use(("sk", h), [0, 1], "v")
            use(("so", h), [2, 3], "v")
            use(("sot", h), [6], "v")

        for h in range(HG):
            use_dense(("f", h))
            if h == 0:
                use_sums("stat_mix")
            if h:
                plan_turn(h - 1)
            use_dense(("g", h))
            if h:
                plan_turn_keys_of(h - 1)
                plan_u(h - 1, 0)
            use_dense(("q", h))
            if h:
                plan_o(h - 1, 0), plan_u(h - 1, 1)
            use_dense(("i", h))
            if h:
                plan_o(h - 1, 1), plan_samp(h - 1)
        plan_turn(HG - 1), plan_turn_keys_of(HG - 1), plan_u(HG - 1, 0)
        plan_o(HG - 1, 0), plan_u(HG - 1, 1), plan_o(HG - 1, 1), plan_samp(HG - 1)

        for c in range(KV):
            use_dense(("ckv", c))
        use_dense("kr")
        use_dense("stat_kv", "s")
        for c in range(KQ):
            use_dense(("cq", c))
        for h in range(H):
            use_dense(("uq", h))
            if h == 0:
                use_sums("stat_q")
        for n in range(NT):
            use(("v", n), [6 + n % 2], "s")
        for p2 in range(H // 2):
            use_dense(("uk", p2), "s")
        for n in range(0, NT, 2):
            use(("ckvo", n), [6], "v")
        use("kro", [7], "s")
        use("ckvs", [6], "v")
        use("krs", [7], "s")
        units = [(q, h) for q in range(NT) for h in range(H)]

        def plan_s(u):
            q, h = u
            use(("S", u), [2 * (h % 2)] if q < 4 else [2 * (h % 2), 2 * (h % 2) + 1], "s")

        plan_s(units[0]), plan_s(units[1])
        for n, u in enumerate(units):
            for half in range(1 if u[0] < 4 else 2):
                use(("pt", u, half), [4 + half], "sv"[half])
            if n + 2 < len(units):
                plan_s(units[n + 2])
            if u[1] % 2 == 0:
                use_o = [6 + u[1] // 2 % 2]
            else:
                use(("po", u[0], u[1] // 2), use_o, "s")

        for n in range(4):
            use(("wk", n), [n], "sv"[n % 2])
        use("qlat", [4], "v")

        def plan_turn_keys(g, first, last):
            for j in range(first, last):
                for c in range(KV):
                    use(("kt", g, j, c), [2 * (j % 2) + c], "sv"[c])
            if last == 4:
                use(("krt", g), [4], "s")

        plan_turn_keys(0, 0, 4)
        for g in range(GT):
            use(("gs", g), [5], "s")
            if g + 1 < GT:
                plan_turn_keys(g + 1, 0, 3)
            use(("gpt", g), [6], "v")
            if g + 1 < GT:
                plan_turn_keys(g + 1, 3, 4)
            use(("go", g), [7], "s")
        use("m1", [0], "v")
        use("snew", [1], "v")
        use("m2", [2], "v")
        use("fin", [3], "v")
        use("oT", [4], "v")
        for c in range(KD):
            use_dense(("out", c))
        for h in range(MH):
            use_dense(("mq", h))
            if h == 0:
                use_sums("stat_memx")
                for m in range(2):
                    for half in range(2):
                        use(("mx", m, half), [6 + half], "sv"[half])
        use("stat_mem", [6], "s")
        for n, name in enumerate(("mk", "mv")):
            for h in range(MH):
                use((name, h), [(4 * n + h) % 6], "v")
        for m in range(2):
            use(("mko", m), [6 + m], "s")
        for m in range(2):
            use(("mvt", m), [m], "s")
        use("qs", [2], "v")
        munits = [(q, hp) for q in range(NT) for hp in range(MH // 2)]

        def plan_ms(n):
            use(("ms", n), [n % 2], "s")

        plan_ms(0), plan_ms(1)
        for n in range(len(munits)):
            use(("mpt", n), [2 + n % 2], "s")
            if n + 2 < len(munits):
                plan_ms(n + 2)
            use(("mpo", n), [4 + n % 2], "v")
            if n % 2 == 0:
                use(("qb", n // 2), [6], "v")
        use("sct", [6], "s")
        use("spt", [7], "v")
        use("spv", [0, 1], "v")
        use("spo", [4], "v")
        for c in range(KD):
            use_dense(("mo", c))
        for kind, what in ffn_order():
            if kind == "up":
                use_dense(("a", what))
                if what == 0:
                    use_sums("stat_ffn")
                use_dense(("b", what))
            else:
                if what == (len(FPARTS) - 1, 0):
                    for f in range(0, NF, 4):
                        use(("tail", f), [6 + f // 4 % 2], "s")
                use_dense(("down", *what))
        use("rtok", [6], "s")
        for n in range(NT + 1):
            for half in range(2):
                use(("y", n, half), [(2 * n + half) % 6], "sv"[half])

        x_dram = i["x_prompt"][0].rearrange("(n p) d -> n p d", p=P)
        xs_dram = i["x_sample"].rearrange("b t d -> (b t) d")
        CONSTS = 1 + 4 + 9 + 2 + 2

        def load_weight(sp, j):
            if j >= 2:
                sp.wait_ge(w_split, j - 1)
            for c0, src in jobs[j][2]:
                m = src.shape[-1]
                sp.dma_start(wtile(wraw, j)[:, :, c0:c0 + m], src).then_inc(w_in_sem[j % 2], 16)

        w_count = []
        for j in range(len(jobs)):
            w_count.append(16 * len(jobs[j][2]) + (w_count[j - 2] if j >= 2 else 0))

        def load_x(sp, n):
            if n >= 4:
                emptied_at = n - 4
                full(sp, ("x", emptied_at, 1))
            if n < NT:
                sp.dma_start(xstage[n % 4][:, :], x_dram[n]).then_inc(x_in[n % 4], 16)
            else:
                sp.dma_start(xstage[n % 4][0:NS, :], xs_dram).then_inc(x_in[n % 4], 16)

        block = ctx.enter_context(nc.Block())

        @block.sync
        def _(sp):
            sp.dma_start(ident[:, :], i["ident"]).then_inc(ident_in, 16)
            for n in range(4):
                load_x(sp, n)
            sp.dma_start(selv[:, :, :, :], i["selv"].rearrange("p (n h b) -> p n h b", n=2, h=MH)).then_inc(consts_in, 16)
            for dst, src in ((sel, i["sel"]), (rowof, i["rowof"]), (causal, i["causal"]), (hmask, i["hmask"])):
                sp.dma_start(dst[:, :], src).then_inc(consts_in, 16)
            row = 0
            for name, n in (("norm_mix", 8), ("norm_memx", 8), ("norm_mem", 8), ("norm_ffn", 8), ("norm_final", 8),
                            ("norm_q", 3), ("norm_kv", 2), ("norm_hg", 1), ("hg_lb_raw", 8)):
                src = i[name] if name == "norm_final" else i[name].rearrange("a c -> (a c)")
                sp.dma_start(crow[row:row + n, :], src.rearrange("(k p) -> k p", p=P)).then_inc(consts_in, 16)
                row += n
            sp.dma_start(cvrow[0:66, :], i["conv_w"].rearrange("a t (k p) -> (a t k) p", p=P)).then_inc(consts_in, 16)
            sp.dma_start(cvrow[66:88, :], i["conv_b"].rearrange("a (k p) -> (a k) p", p=P)).then_inc(consts_in, 16)
            sp.dma_start(scrow[:, :], i["state_conv"][0].rearrange("b t f -> (b t) f")).then_inc(consts_in, 16)
            sp.dma_start(OTMP[0:GT, 0, 0:GP].bitcast(I32), i["page_table"].rearrange("b (g j) -> (b g) j", j=GP)).then_inc(consts_in, 16)
            load_weight(sp, 0), load_weight(sp, 1)
            for n in range(4, NT + 1):
                load_x(sp, n)
            sp.dma_start(o["conv_sample"][0, :, 0], i["state_conv"][0, :, 1]).then_inc(cs_out, 16)
            for j in range(2, len(jobs)):
                load_weight(sp, j)
                if j % 4 == 1 and 0 < j <= 4 * HG + 1:
                    h = j // 4 - 1
                    if h:
                        sp.wait_ge(sb_out, 16 * h)
                        full(sp, ("so", h - 1))
                    sp.dma_start(SB[:, :, :], i["state_hgrn"][0, :, h].rearrange("b k v -> k b v")).then_inc(sb_in, 16)
                if j == job_no["kr"]:
                    full(sp, ("tk", HG - 1, 1))
                    sp.dma_start(trig[0:64, :], i["trig"]).then_inc(trig_in, 16)
                if j == job_no[("out", 1)]:
                    full(sp, ("uq", H - 1))
                    sp.wait_ge(q_new, H)
                    sp.dma_start(wuk[:, :, :], cols(w_uk, 0, H * NOPE)).then_inc(wuk_in, 16)
                if j == job_no[("mq", 0)]:
                    full(sp, ("out", KD - 1))
                    for m in range(2):
                        sp.dma_start(mraw[m][:, :], i["mem_prompt"][0, m * P:m * P + P]).then_inc(mem_in, 16)
                if j == job_no[("mv", 3)]:
                    full(sp, ("mq", MH - 1))
                    for b in range(NS):
                        sp.dma_start(sV[b][:, :, :], i["cache_mem_v"][0, b].rearrange("(t p) h e -> p t (h e)", p=P)).then_inc(sv_in, 16)
                        if b >= 2:
                            emptied(sp, ("qb", b - 2))
                        sp.dma_start(sK[b % 2][:, :, :], i["cache_mem_k"][0, b].rearrange("(t p) h e -> p t (h e)", p=P)).then_inc(sk_in[b % 2], 16)
                if j == job_no[("uq", 2)]:
                    sp.wait_ge(rstd_new, 3)
                    sp.dma_start(wuv[:, :, :], cols(w_uv, 0, H * VD)).then_inc(wuv_in, 16)
            for n in range(NT + 1):
                emptied(sp, ("y", n, 0)), emptied(sp, ("y", n, 1))
                if n < NT:
                    sp.dma_start(o["y_prompt"][0, n * P:n * P + P], yst[n % 4][:, :]).then_inc(y_out[n % 4], 16)
                else:
                    sp.dma_start(o["y_sample"][:, 0], yst[n % 4][0:NS, :]).then_inc(y_out[n % 4], 16)
            for n in range(4):
                sp.wait_ge(y_out[n], 16 * len(range(n, NT + 1, 4)))
            for sm, n in ((sb_out, HG), (hst_out, HG), (ckv_out, 2), (kr_out, 2), (mk_out, 1), (mv_out, 1), (tail_out, 2), (cs_out, 1)):
                sp.wait_ge(sm, 16 * n)

        @block.gpsimd
        def _(gp):
            steps = [0]

            def step(ins):
                steps[0] += 1
                ins.then_inc(pstep, 1)
                gp.wait_ge(pstep, steps[0])

            def split_weight(j):
                k = jobs[j][1]
                gp.wait_ge(w_in_sem[j % 2], w_count[j])
                if j >= 2:
                    full(gp, jobs[j - 2][0])
                hi, lo, raw = (r[j % 2][:, 0:k * P] for r in (whi, wlo, wraw))
                gp.tensor_copy(hi, raw).then_inc(w_hi_done, 1)
                gp.wait_ge(w_hi_done, j + 1)
                gp.tensor_tensor(lo, raw, hi, ALU.subtract).then_inc(w_split, 1)

            def spread_v(h, half):
                emptied(gp, ("tv", h, half))
                if half:
                    full(gp, ("u", h, 0, 3))
                elif h:
                    full(gp, ("u", h - 1, 1, 3))
                for c in range(4):
                    r = slice(32 * c, 32 * c + 32)
                    ins = gp.tensor_copy(v4[r, :, c, :], vtok[r, 4 * half:4 * half + 4, :])
                    if c < 3:
                        step(ins)
                ins.then_inc(v4_new, 1)
                gp.wait_ge(v4_new, 2 * h + half + 1)

            ckv_rows = i["cache_ckv"][0].rearrange("n (a t) l -> (n a) (t l)", t=GP)
            kr_rows = i["cache_krope"][0].rearrange("n (a t) r -> (n a) (t r)", t=GP)

            def load_pages(g):
                if g == 0:
                    emptied(gp, "idx")
                full(gp, ("go", g - 3) if g >= 3 else ("po", NT - 1, H // 2 - 1))
                at_ = bass.IndirectOffsetOnAxis(ap=idx[:, g:g + 1].bitcast(U32), axis=0)
                for dst, rows in ((rc, ckv_rows), (rk, kr_rows)):
                    gp.indirect_dma_start(out=dst[g % 3][:, :, :].rearrange("p t l -> p (t l)"), out_offset=None, in_=rows,
                                          in_offset=at_).then_inc(page_in[g % 3], 16)

            gp.memset(ones[:, :], 1.0).then_inc(ones_set, 1)
            gp.memset(eps[:, :], EPS).then_inc(ones_set, 1)
            step(gp.memset(v4[:, :, :, :], 0.0))
            spread_behind = {job_no[(name, h + 1)]: [(h, half)] for h in range(HG - 1) for half, name in enumerate("qi")}
            spread_behind[job_no[("ckv", 1)]] = [(HG - 1, 0), (HG - 1, 1)]
            for j in range(len(jobs)):
                split_weight(j)
                if j == job_no[("out", 1)]:
                    for g in range(GT):
                        load_pages(g)
                for h, half in spread_behind.get(j, ()):
                    gp.wait_ge(w_split, j + 1)
                    spread_v(h, half)

        @block.tensor
        def _(pe):
            def begin(key):
                for by, n in uses[key][4]:
                    pe.wait_ge(freed[by], n)

            def end(ins):
                ins.then_inc(psum_full, 1)

            def dense(name, hi, lo, ready, n=CH, m=P, order=None, tile=lambda t: t):
                j, k = job_no[name], jobs[job_no[name]][1]
                begin(name)
                pe.wait_ge(w_split, j + 1)
                wh, wl = wtile(whi, j), wtile(wlo, j)
                for t in order or range(k):
                    ready(t)
                    for c in range(len(uses[name][1])):
                        out, s = bank(name, c)[0:m, 0:n], slice(c * n, c * n + n)
                        first, last = (order or range(k))[0], (order or range(k))[-1]
                        pe.matmul(out, wh[:, t, 0:m], hi[:, tile(t), s], start=(t == first), stop=False)
                        pe.matmul(out, wh[:, t, 0:m], lo[:, tile(t), s], start=False, stop=False)
                        ins = pe.matmul(out, wl[:, t, 0:m], hi[:, tile(t), s], start=False, stop=(t == last))
                end(ins)

            def column_sums(key, src):
                begin(key)
                for c in range(NCH):
                    ins = pe.matmul(bank(key, c)[:, 0:CH], ones[:, :], src[:, c * CH:c * CH + CH], start=True, stop=True)
                end(ins)

            def turn(key, tiles, rows=P):
                begin(key)
                at_ = 0
                for tile in tiles:
                    w = tile.shape[0]
                    ins = pe.transpose(bank(key)[0:tile.shape[1], at_:at_ + w], tile, ident[0:w, 0:w])
                    at_ += w
                end(ins)

            pe.wait_ge(ident_in, 16)
            for n in range(NT + 1):
                if n == 4:
                    pe.wait_ge(consts_in, 16 * CONSTS)
                    turn("cst", [crow[:, :], cvrow[:, :]])
                    turn("scv", [scrow[:, f * P:f * P + P] for f in range(NF)])
                    pe.wait_ge(pg_new, 1)
                    turn("idx", [SB[0:GT, 0, :]])
                w = P if n < NT else NS
                pe.wait_ge(x_in[n % 4], 16 * (n // 4 + 1))
                for half in range(2):
                    turn(("x", n, half), [xstage[n % 4][0:w, (4 * half + k) * P:(4 * half + k + 1) * P] for k in range(4)])
            pe.wait_ge(ones_set, 2)

            def mix_ready(k):
                pe.wait_ge(lo_done, k + 1)

            def hg_turn(h):
                emptied(pe, ("i", h))
                for half in range(2):
                    turn(("tv", h, half), [v0[:, (4 * half + n) * P:(4 * half + n + 1) * P] for n in range(4)])
                begin(("ts", h))
                pe.transpose(bank(("ts", h))[0:NS, 0:P], rows_of(h)[:, 0:NS], ident[:, :])
                end(pe.transpose(bank(("ts", h))[0:NS, P:2 * P], v0[:, T:TT], ident[:, :]))

            def hg_turn_keys(h):
                pe.wait_ge(qk_new, h + 1)
                for half in range(2):
                    turn(("tk", h, half), [t2[:, (4 * half + n) * P:(4 * half + n + 1) * P] for n in range(4)])

            def hg_update(h, half):
                emptied(pe, ("tk", h, half))
                pe.wait_ge(v4_new, 2 * h + half + 1)
                for n in range(4):
                    key = ("u", h, half, n)
                    begin(key)
                    end(pe.matmul(bank(key), ketok[:, 4 * half + n, :], v4[:, n, :, :].rearrange("p c v -> p (c v)"),
                                  start=True, stop=True))
                key = ("a", h, half)
                begin(key)
                for n in range(4):
                    s = slice((4 * half + n) * P, (4 * half + n + 1) * P)
                    ins = pe.matmul(bank(key)[:, n * P:n * P + P], t1[:, s], tq[h % 2][:, s], start=True, stop=True)
                end(ins)

            def hg_out(h, half):
                key = ("o", h, half)
                begin(key)
                emptied(pe, ("a", h, half))
                emptied(pe, ("u", h, half, 3))
                for n in range(4):
                    c0 = n * P
                    pe.matmul(bank(key)[:, c0:c0 + P], AT[:, n, :], vtok[:, 4 * half + n, :], start=True, stop=False,
                              skip_group_check=True)
                    for c in range(4):
                        q = tq[h % 2][:, (4 * half + n) * P + CK * c:(4 * half + n) * P + CK * (c + 1)]
                        ins = pe.matmul(PS[32 * c:32 * c + 32, uses[key][1][0], c0:c0 + P], q, Sst[:, 4 * n + c, :],
                                        start=False, stop=(c == 3), skip_group_check=True)
                end(ins)
                emptied(pe, key)
                turn(("ot", h, half), [ON[:, n, :] for n in range(4)])

            def hg_sample(h):
                key = ("sk", h)
                emptied(pe, ("ts", h))
                begin(key)
                for n in range(2):
                    ins = pe.matmul(bank(key, n), small[0:NS, :], OTMP[0:NS, 4 * n:4 * n + 4, :].rearrange("p b v -> p (b v)"),
                                    start=True, stop=True)
                end(ins)
                emptied(pe, key)
                key = ("so", h)
                begin(key)
                for n in range(2):
                    ins = pe.matmul(bank(key, n)[0:NS, :], tq[h % 2][:, T:TT], SB[:, 4 * n:4 * n + 4, :].rearrange("p b v -> p (b v)"),
                                    start=True, stop=True)
                end(ins)
                pe.wait_ge(os_new, h + 1)
                turn(("sot", h), [OTMP[0:NS, 0, :]])

            for h in range(HG):
                dense(("f", h), XH, XL, mix_ready)
                if h == 0:
                    pe.wait_ge(ss_done, KD - 1)
                    column_sums("stat_mix", SS)
                if h:
                    hg_turn(h - 1)
                dense(("g", h), XH, XL, mix_ready)
                if h:
                    hg_turn_keys(h - 1)
                    hg_update(h - 1, 0)
                dense(("q", h), XH, XL, mix_ready)
                if h:
                    hg_out(h - 1, 0)
                    hg_update(h - 1, 1)
                dense(("i", h), XH, XL, mix_ready)
                if h:
                    hg_out(h - 1, 1)
                    hg_sample(h - 1)
            hg_turn(HG - 1)
            hg_turn_keys(HG - 1)
            hg_update(HG - 1, 0)
            hg_out(HG - 1, 0)
            hg_update(HG - 1, 1)
            hg_out(HG - 1, 1)
            hg_sample(HG - 1)

            for c in range(KV):
                dense(("ckv", c), XH, XL, mix_ready)
            dense("kr", XH, XL, mix_ready)
            pe.wait_ge(kv_sum, 1)
            column_sums("stat_kv", SS)
            for c in range(KQ):
                dense(("cq", c), XH, XL, mix_ready)
            for h in range(H):
                dense(("uq", h), cqh, cql, lambda t: pe.wait_ge(lo_done, hi_before["q"] + t + 1))
                if h == 0:
                    pe.wait_ge(ss_done, ss_before["q"] + KQ - 1)
                    column_sums("stat_q", SS)
            pe.wait_ge(wuv_in, 16)
            for n in range(NT):
                key = ("v", n)
                begin(key)
                for c in range(KV):
                    ins = pe.matmul(bank(key), ckvT[:, c, n * P:n * P + P], wuv[:, c, :], start=(c == 0), stop=(c == KV - 1))
                end(ins)
            for p2 in range(H // 2):
                dense(("uk", p2), ckh, ckl, lambda t: pe.wait_ge(kv_lo, t + 1))
            for n in range(0, NT, 2):
                turn(("ckvo", n), [ckvT[:, c, m * P:m * P + P] for m in (n, n + 1) for c in range(KV)])
            begin("kro")
            for n in range(NT):
                ins = pe.transpose(bank("kro")[:, n * ROPE:n * ROPE + ROPE], trig[96:P, n * P:n * P + P], ident[96:P, 96:P])
            end(ins)
            turn("ckvs", [ckvT[:, c, T:TT] for c in range(KV)])
            begin("krs")
            end(pe.transpose(bank("krs")[0:NS, 0:ROPE], trig[96:P, T:TT], ident[96:P, 96:P]))

            def attention_scores(u):
                q, h = u
                key = ("S", u)
                begin(key)
                w = (q + 1) * P
                for c0 in range(0, w, 512):
                    c1 = min(w, c0 + 512)
                    ins = pe.matmul(bank(key, c0 // 512)[:, 0:c1 - c0], qT[0:QK, h, q * P:q * P + P], kT[0:QK, h, c0:c1],
                                    start=True, stop=True)
                end(ins)

            def turn_probabilities(n, u):
                q, h = u
                pe.wait_ge(p_new, n + 1)
                halves = 1 if q < 4 else 2
                for half in range(halves):
                    turn(("pt", u, half), [Pr[n % 2][:, m * P:m * P + P] for m in range(4 * half, min(q + 1, 4 * half + 4))])

            def attention_values(n, u):
                q, h = u
                key = ("po", q, h // 2)
                if h % 2 == 0:
                    begin(key)
                for m in range(q + 1):
                    if m % 4 == 0:
                        emptied(pe, ("pt", u, m // 4))
                    r = 64 * (h % 2)
                    ins = pe.matmul(PS[r:r + 64, uses[key][1][0], 0:P], V[:, m, h * VD:h * VD + VD], PTr[n % 2][:, m, :],
                                    start=(m == 0), stop=(m == q), skip_group_check=True)
                if h % 2:
                    end(ins)
                else:
                    ins.then_inc(even_done, 1)

            emptied(pe, ("uk", H // 2 - 1))
            pe.wait_ge(krk_new, 1)
            pe.wait_ge(q_new, H)
            attention_scores(units[0])
            attention_scores(units[1])
            for n, u in enumerate(units):
                turn_probabilities(n, u)
                if n + 2 < len(units):
                    attention_scores(units[n + 2])
                attention_values(n, u)

            pe.wait_ge(wuk_in, 16)
            for n in range(4):
                turn(("wk", n), [wuk[:, c, (2 * n + hh) * NOPE:(2 * n + hh + 1) * NOPE] for hh in range(2) for c in range(KV)])
            begin("qlat")
            for n in range(4):
                emptied(pe, ("wk", n))
            for c in range(KV):
                for h in range(H):
                    ins = pe.matmul(bank("qlat")[:, c * 64 + h * NS:c * 64 + h * NS + NS], wukT[0:NOPE, h, c * P:c * P + P],
                                    small[0:NOPE, 24 + h * NS:24 + h * NS + NS], start=True, stop=True)
            end(ins)

            def turn_keys(g, first, last):
                s = g % 3
                pe.wait_ge(page_in[s], 32 * (g // 3 + 1))
                for j in range(first, last):
                    for c in range(KV):
                        turn(("kt", g, j, c), [rc[s][:, 4 * j + n, c * P:c * P + P] for n in range(4)])
                if last == 4:
                    turn(("krt", g), [rk[s][:, 4 * j:4 * j + 4, :].rearrange("p t r -> p (t r)") for j in range(4)])

            def group_scores(g):
                key, b = ("gs", g), g // NG
                begin(key)
                for j in range(4):
                    for c in range(KV):
                        emptied(pe, ("kt", g, j, c))
                emptied(pe, ("krt", g))
                k = uses[key][1][0]
                for c in range(KV):
                    for j in range(4):
                        pe.matmul(PS[32 * j:32 * j + 32, k, :], qlat[:, c, b, :], KT[:, j, c, :], start=(c == 0), stop=False,
                                  skip_group_check=True)
                for n in range(4):
                    for j in range(4):
                        ins = pe.matmul(PS[32 * j:32 * j + 32, k, n * P:n * P + P], qrz[:, b, n, :], KRT[:, j, :], start=False,
                                        stop=(n == 3), skip_group_check=True)
                end(ins)

            def turn_weights(g):
                emptied(pe, ("gs", g))
                turn(("gpt", g), [Ps[g % 2][:, n * P:n * P + P] for n in range(4)])

            def group_values(g):
                key = ("go", g)
                begin(key)
                emptied(pe, ("gpt", g))
                k = uses[key][1][0]
                for n in range(4):
                    for j in range(4):
                        ins = pe.matmul(PS[32 * j:32 * j + 32, k, 0:KVL], PTs[:, n, 32 * j:32 * j + 32], rc[g % 3][:, 4 * j + n, :],
                                        start=(n == 0), stop=(n == 3), skip_group_check=True)
                end(ins)

            turn_keys(0, 0, 4)
            emptied(pe, "qlat")
            pe.wait_ge(qz_new, 1)
            for g in range(GT):
                group_scores(g)
                if g + 1 < GT:
                    turn_keys(g + 1, 0, 3)
                turn_weights(g)
                if g + 1 < GT:
                    turn_keys(g + 1, 3, 4)
                group_values(g)
            pe.wait_ge(seq_o, NS)
            turn("m1", [nmS])
            begin("snew")
            for c in range(KV):
                pe.matmul(bank("snew")[0:NS, 0:256], small[:, 8 * c:8 * c + 8], qlat[:, c, :, :].rearrange("p b h -> p (b h)"),
                          start=(c == 0), stop=False, skip_group_check=True)
            end(pe.matmul(bank("snew")[0:NS, 0:256], krs0, qrz[0:ROPE, :, 0, :], start=False, stop=True, skip_group_check=True))
            pe.wait_ge(c_diff, 1)
            turn("m2", [expd])
            pe.wait_ge(ls_new, 1)
            begin("fin")
            fin = bank("fin")
            pe.matmul(fin[:, 0:64], ones[:, :], LS, start=True, stop=False, skip_group_check=True)
            pe.matmul(fin[:, 0:64], ones[0:NS, :], WD, start=False, stop=True, skip_group_check=True)
            pe.matmul(fin[:, 64:128], ones[0:NS, :], WD, start=True, stop=True, skip_group_check=True)
            for c in range(KV):
                for b in range(NS):
                    ins = pe.matmul(fin[:, P + c * 64 + b * H:P + c * 64 + b * H + H], Oacc[:, b, c * P:c * P + P], sel[:, :],
                                    start=True, stop=True, skip_group_check=True)
            end(ins)
            pe.wait_ge(lat_new, 1)
            begin("oT")
            for p2 in range(H // 2):
                for c in range(KV):
                    ins = pe.matmul(bank("oT")[:, p2 * 16:p2 * 16 + 16], wuv[:, c, p2 * P:p2 * P + P], lat[:, c, :, 2 * p2:2 * p2 + 2],
                                    start=(c == 0), stop=(c == KV - 1))
            end(ins)

            order = [4, 5, 6, 7, 0, 1, 2, 3]
            for c in range(KD):
                dense(("out", c), CHi, CLo, lambda t: pe.wait_ge(cat_lo, order.index(t) + 1), order=order)
            for h in range(MH):
                dense(("mq", h), BH, BL, lambda t: pe.wait_ge(lo_done, hi_before["memx"] + t + 1))
                if h == 0:
                    pe.wait_ge(ss_done, ss_before["memx"] + KD - 1)
                    column_sums("stat_memx", SS)
                    pe.wait_ge(mem_in, 32)
                    for m in range(2):
                        for half in range(2):
                            turn(("mx", m, half), [mraw[m][:, (4 * half + k) * P:(4 * half + k + 1) * P] for k in range(4)])
            pe.wait_ge(ss_done, ss_before["mem"] + KD - 1)
            begin("stat_mem")
            end(pe.matmul(bank("stat_mem")[:, 0:MT], ones[:, :], SS[:, 0:MT], start=True, stop=True))
            for name in ("mk", "mv"):
                for h in range(MH):
                    dense((name, h), mh, ml, lambda t: pe.wait_ge(lo_done, hi_before["mem"] + t + 1), n=MT)
            for m in range(2):
                emptied(pe, ("mk", MH - 1))
                turn(("mko", m), [MKT[:, h, m * P:m * P + P] for h in range(MH)])
            for m in range(2):
                emptied(pe, ("mv", MH - 1))
                turn(("mvt", m), [mvT[:, h, m * P:m * P + P] for h in range(MH)])
            begin("qs")
            for h in range(MH):
                ins = pe.transpose(bank("qs")[0:NS, h * P:h * P + P], qm[:, h, T:TT], ident[:, :])
            end(ins)

            def memory_scores(n):
                q, hp = munits[n]
                key = ("ms", n)
                begin(key)
                for hh in range(2):
                    h = 2 * hp + hh
                    ins = pe.matmul(bank(key)[:, hh * MT:hh * MT + MT], qm[:, h, q * P:q * P + P], MKT[:, h, :], start=True, stop=True)
                end(ins)

            memory_scores(0)
            memory_scores(1)
            for n, (q, hp) in enumerate(munits):
                pe.wait_ge(m_new, n + 1)
                turn(("mpt", n), [Pm[n % 2][:, hh, m * P:m * P + P] for hh in range(2) for m in range(2)])
                if n + 2 < len(munits):
                    memory_scores(n + 2)
                key = ("mpo", n)
                begin(key)
                emptied(pe, ("mpt", n))
                for hh in range(2):
                    for m in range(2):
                        h = 2 * hp + hh
                        ins = pe.matmul(bank(key)[:, hh * P:hh * P + P], MV[:, m, h * P:h * P + P], PTm[n % 2][:, 2 * hh + m, :],
                                        start=(m == 0), stop=(m == 1))
                end(ins)
                if n % 2 == 0:
                    b = n // 2
                    pe.wait_ge(qs_set, 1)
                    begin(("qb", b))
                    end(pe.matmul(bank(("qb", b)), OH[0:NS, b, :], QS[0:NS, :], start=True, stop=True))
            pe.wait_ge(prod_done, NS)
            begin("sct")
            for m in range(2):
                ins = pe.transpose(bank("sct")[0:32, m * P:m * P + P], sc[:, m, :], ident[:, :])
            end(ins)
            pe.wait_ge(s_new2, 1)
            turn("spt", [scr[0:32, m * P:m * P + P] for m in range(2)])
            emptied(pe, "spt")
            pe.wait_ge(sv_in, 16 * NS)
            begin("spv")
            for m in range(2):
                for b in range(NS):
                    r = 32 * (b % 4)
                    ins = pe.matmul(PS[r:r + 32, uses["spv"][1][b // 4], :], pm[:, m, :], sV[b][:, m, :],
                                    start=(m == 0), stop=(m == 1), skip_group_check=True)
            end(ins)
            emptied(pe, "spv")
            begin("spo")
            for h in range(MH):
                for half in range(2):
                    ins = pe.matmul(bank("spo")[:, NS * h + 4 * half:NS * h + 4 * half + 4], prod[:, half, h * P:h * P + P],
                                    selv[:, half, h, :], start=True, stop=True)
            end(ins)
            emptied(pe, "spo")
            for c in range(KD):
                dense(("mo", c), omh, oml, lambda t: None)
            for kind, what in ffn_order():
                if kind == "up":
                    for name in ("a", "b"):
                        dense((name, what), BH, BL, lambda t: pe.wait_ge(lo_done, hi_before["ffn"] + t + 1))
                        if (name, what) == ("a", 0):
                            pe.wait_ge(ss_done, ss_before["ffn"] + KD - 1)
                            column_sums("stat_ffn", SS)
                else:
                    part = FPARTS[what[0]]
                    if what == (len(FPARTS) - 1, 0):
                        emptied(pe, ("b", NF - 1))
                        for f in range(0, NF, 4):
                            turn(("tail", f), [atail[:, k, :] for k in range(f, min(f + 4, NF))])
                    dense(("down", *what), acth, actl, lambda t: pe.wait_ge(act_lo, part[t] + 1), tile=lambda t: part[t] % FSLOTS)
            pe.wait_ge(ss_done, ss_before["final"] + KD - 1)
            begin("rtok")
            for n in range(NT + 1):
                w = P if n < NT else NS
                ins = pe.matmul(bank("rtok")[0:w, n:n + 1], SS[:, n * P:n * P + w], ones[:, 0:1], start=True, stop=True)
            end(ins)
            for n in range(NT + 1):
                w = P if n < NT else NS
                for half in range(2):
                    key = ("y", n, half)
                    begin(key)
                    for k in range(4):
                        pe.wait_ge(hi_done, hi_before["final"] + 4 * half + k + 1)
                        ins = pe.transpose(bank(key)[0:w, k * P:k * P + P], XG[:, 4 * half + k, n * P:n * P + w], ident[:, :])
                    end(ins)

        @block.scalar
        def _(act):
            steps = [0]

            def step(ins):
                steps[0] += 1
                ins.then_inc(sstep, 1)
                act.wait_ge(sstep, steps[0])

            def rstd_rows(key, out, width):
                full(act, key)
                if key == "stat_mem":
                    src, var = bank(key)[:, 0:MT], SS[:, 0:MT]
                else:
                    src, var, = chunks(key), by3(SS[:, :])
                    out = by3(out)
                act.activation(var, src, ACT.Identity, bias=eps[:, 0:1], scale=1.0 / width)
                step(act.activation(out, src, ACT.Ln, bias=eps[:, 0:1], scale=1.0 / width))
                act.activation(out, out, ACT.Exp, scale=-0.5).then_inc(freed["s"], 1)

            def rstd(out, src, width, done):
                step(act.activation(out, src, ACT.Ln, bias=eps[0:out.shape[0], 0:1], scale=1.0 / width))
                act.activation(out, out, ACT.Exp, scale=-0.5).then_inc(done, 1)

            def split_and_square(stage, gain, src, hi, ready, n):
                for k in range(n):
                    ready(k)
                    act.activation(hi[:, k, :], src[:, k, :], ACT.Copy, scale=gains[:, gain + k:gain + k + 1]).then_inc(hi_done, 1)
                    if k:
                        if k > 1:
                            act.wait_ge(ss_done, ss_before[stage] + k - 1)
                        act.activation(SQ[:, 0:src.shape[2]], src[:, k, :], ACT.Square).then_inc(sq_done, 1)
                    else:
                        act.activation(SS[:, 0:src.shape[2]], src[:, k, :], ACT.Square).then_inc(sq_done, 1)

            act.preload_act_table_set("natural_log_exp_and_others")
            for n in range(NT + 1):
                if n == 4:
                    act.wait_ge(lb_diff, 1)
                    act.activation(lbt[:, 4:12], lbt[:, 4:12], ACT.Exp).then_inc(lb_exp, 1)
                w = P if n < NT else NS
                key = ("x", n, 0)
                full(act, key)
                act.activation(XT[:, 0:4, n * P:n * P + w], bank(key)[:, 0:4 * w].rearrange("p (k t) -> p k t", k=4),
                               ACT.Copy).then_inc(freed["s"], 1)

            def x_ready(k):
                emptied(act, ("x", NT, k // 4))

            split_and_square("mix", 0, XT, XH, x_ready, KD)
            rstd_rows("stat_mix", RB1[:, :], D)

            def o_squares(h, half):
                full(act, ("o", h, half))
                prev = 2 * h + half - 1
                if prev >= 0:
                    full(act, ("ot", prev // 2, prev % 2))
                act.activation(ON[:, :, :].rearrange("p n v -> p (n v)"), bank(("o", h, half)), ACT.Square).then_inc(o_sq, 1)
                act.wait_ge(o_ms, 2 * h + half + 1)
                rstd(smp[:, 20:24], smp[:, 16:20], DK, o_rstd)

            def turned_out(h, name, dst):
                for half in range(2):
                    key = (name, h, half)
                    full(act, key)
                    act.activation(dst[:, 4 * half:4 * half + 4, :].rearrange("p n v -> p (n v)"), bank(key),
                                   ACT.Copy).then_inc(freed["s"], 1)

            def states_out(h):
                emptied(act, ("u", h, 1, 3))
                act.dma_start(o["hgrn_prompt"][0, 0, h], Sst[:, 16, :]).then_inc(hst_out, 16)

            def sample_state_out(h):
                emptied(act, ("sk", h))
                act.dma_start(o["hgrn_sample"][0, :, h].rearrange("b k v -> k b v"), SB[:, :, :]).then_inc(sb_out, 16)
                act.wait_ge(os_ms, h + 1)
                rstd(OTMP[0:NS, 2, 1:2], OTMP[0:NS, 2, 0:1], DK, os_rstd)

            for h in range(HG):
                if h:
                    turned_out(h - 1, "tv", vtok)
                act.wait_ge(f_raw, h + 1)
                act.activation(t0[:, :], t0[:, :], ACT.Exp, scale=-1.0).then_inc(f_exp, 1)
                if h:
                    turned_out(h - 1, "tk", ketok)
                act.wait_ge(g_raw, h + 1)
                act.activation(v0[:, :], v0[:, :], ACT.Exp, scale=-1.0).then_inc(g_exp, 1)
                act.wait_ge(f_new, h + 1)
                act.activation(t2[:, 0:T], t0[:, 0:T], ACT.Ln).then_inc(f_log, 1)
                if h:
                    o_squares(h - 1, 0)
                act.wait_ge(b_new, h + 1)
                act.activation(t2[:, 0:T], t0[:, 0:T], ACT.Exp).then_inc(b_exp, 1)
                act.activation(t0[:, 0:T], t0[:, 0:T], ACT.Exp, scale=-1.0).then_inc(b_nexp, 1)
                if h:
                    o_squares(h - 1, 1)
                    states_out(h - 1)
                    sample_state_out(h - 1)
            turned_out(HG - 1, "tv", vtok)
            turned_out(HG - 1, "tk", ketok)
            o_squares(HG - 1, 0)
            states_out(HG - 1)
            o_squares(HG - 1, 1)
            sample_state_out(HG - 1)

            emptied(act, ("sot", HG - 1))
            for c in range(KV):
                emptied(act, ("ckv", c))
                act.activation((SS, SQ)[c][:, :], ckvT[:, c, :], ACT.Square).then_inc(kv_sq, 1)
            act.wait_ge(sb_out, 16 * HG)
            rstd_rows("stat_kv", RB2[:, :], KVL)
            split_and_square("q", 40, cqr, cqh, lambda k: emptied(act, ("cq", k)), KQ)
            rstd_rows("stat_q", RB1[:, :], QL)
            act.wait_ge(krT_new, 1)
            for h in range(H):
                ins = act.activation(kT[NOPE:QK, h, :], trig[96:P, :], ACT.Copy)
            ins.then_inc(krk_new, 1)
            full(act, ("uq", H - 1))
            for c in range(KV):
                act.activation(ckh[:, c, :], ckvT[:, c, :], ACT.Copy).then_inc(kv_hi, 1)
            for n in range(NT):
                full(act, ("v", n))
                act.activation(V[:, n, :], bank(("v", n)), ACT.Copy).then_inc(freed["s"], 1)
            for p2 in range(H // 2):
                key = ("uk", p2)
                full(act, key)
                act.activation(by3(kT[0:NOPE, 2 * p2, :]), chunks(key, 0, 64), ACT.Copy)
                act.activation(by3(kT[0:NOPE, 2 * p2 + 1, :]), chunks(key, 64, P), ACT.Copy).then_inc(freed["s"], 1)
            full(act, "kro")
            act.activation(kro[:, 0:NT, :].rearrange("p n r -> p (n r)"), bank("kro")[:, 0:NT * ROPE], ACT.Copy).then_inc(freed["s"], 1)
            full(act, "krs")
            act.activation(kro[0:NS, NT, :], bank("krs")[0:NS, 0:ROPE], ACT.Copy).then_inc(freed["s"], 1)
            emptied(act, "krs")
            act.dma_start(o["krope_prompt"][0, 0].rearrange("(n p) r -> p n r", p=P), kro[:, 0:NT, :]).then_inc(kr_out, 16)
            act.dma_start(o["krope_sample"][0, :, 0], kro[0:NS, NT, :]).then_inc(kr_out, 16)
            emptied(act, "ckvs")
            act.dma_start(o["ckv_prompt"][0, 0].rearrange("(n p) l -> p n l", p=P), ckvo[:, 0:NT, :]).then_inc(ckv_out, 16)
            act.dma_start(o["ckv_sample"][0, :, 0], ckvo[0:NS, NT, :]).then_inc(ckv_out, 16)

            def exp_scores(n, u):
                q, h = u
                w = (q + 1) * P
                act.wait_ge(p_max, n + 1)
                if n >= 2:
                    full(act, ("pt", units[n - 2], 0 if units[n - 2][0] < 4 else 1))
                b0 = uses[("S", u)][1][0]
                act.activation(Pr[n % 2][:, 0:w], PS[:, b0:b0 + 2, :].rearrange("p b k -> p (b k)")[:, 0:w], ACT.Exp,
                               bias=small[:, 96 + n % 4:97 + n % 4], accum_out=small[:, 100 + n % 4:101 + n % 4]).then_inc(freed["s"], 1)

            emptied(act, "ckvs")
            exp_scores(0, units[0])
            exp_scores(1, units[1])
            for n, u in enumerate(units):
                q, h = u
                m = min(q + 1, 4)
                full(act, ("pt", u, 0))
                if n >= 2:
                    full(act, ("po", units[n - 2][0], units[n - 2][1] // 2)) if units[n - 2][1] % 2 else act.wait_ge(even_done, (n - 2) // 2 + 1)
                act.activation(PTr[n % 2][:, 0:m, :].rearrange("p m q -> p (m q)"), bank(("pt", u, 0))[:, 0:m * P], ACT.Copy).then_inc(freed["s"], 1)
                if n + 2 < len(units):
                    exp_scores(n + 2, units[n + 2])
                if h % 2:
                    key = ("po", q, h // 2)
                    full(act, key)
                    if n == 1:
                        act.wait_ge(kr_out, 32)
                        act.wait_ge(ckv_out, 32)
                    act.activation(MO[:, h // 2, q * P:q * P + P], bank(key)[:, 0:P], ACT.Copy).then_inc(freed["s"], 1)

            def copy_out(key, out, src):
                full(act, key)
                act.activation(out, src, ACT.Copy).then_inc(freed["s"], 1)

            for n in (0, 2):
                copy_out(("wk", n), wukT[0:NOPE, 2 * n:2 * n + 2, :].rearrange("p h l -> p (h l)"), bank(("wk", n))[0:NOPE, :])

            def keys_out(g):
                if g == 0:
                    full(act, "qlat")
                for j in range(4):
                    copy_out(("kt", g, j, 0), KT[:, j, 0, :], bank(("kt", g, j, 0)))
                copy_out(("krt", g), KRT[:, :, :].rearrange("p j k -> p (j k)"), bank(("krt", g)))

            def group_exp(g):
                act.wait_ge(g_max, g + 1)
                if g >= 2:
                    full(act, ("gpt", g - 2))
                act.activation(Ps[g % 2][:, :], bank(("gs", g)), ACT.Exp, bias=nmax[:, g:g + 1], accum_out=lsum[:, g:g + 1])\
                   .then_inc(freed["s"], 1)

            def sequence_weights(b):
                act.wait_ge(seq_w, b + 1)
                act.activation(wgt, nmax[:, NG * b:NG * b + NG], ACT.Exp, bias=nmS[:, b:b + 1], scale=-1.0).then_inc(seq_wd, 1)

            keys_out(0)
            for g in range(GT):
                group_exp(g)
                if g >= NG and g % NG == 0:
                    sequence_weights(g // NG - 1)
                if g + 1 < GT:
                    keys_out(g + 1)
                if g % NG == 0 and g:
                    act.wait_ge(seq_o, g // NG)
                copy_out(("go", g), Og[:, g % NG, :], bank(("go", g))[:, 0:KVL])
            sequence_weights(NS - 1)
            act.wait_ge(c_new, 1)
            act.activation(wnew, wnew, ACT.Exp).then_inc(c_exp, 1)
            act.wait_ge(c_diff, 2)
            act.activation(fac, fac, ACT.Exp).then_inc(c_fac, 1)
            full(act, "oT")
            for n in range(KD):
                t = (n + 4) % KD
                if t == 0:
                    emptied(act, "oT")
                src = MO[:, t, :] if t < 4 else HGO[:, t - 4, :]
                act.activation(CHi[:, t, :], src, ACT.Copy).then_inc(cat_hi, 1)
            split_and_square("memx", 8, XT, BH, lambda k: emptied(act, ("out", k)), KD)
            rstd_rows("stat_memx", RB1[:, :], D)
            for m in range(2):
                key = ("mx", m, 0)
                copy_out(key, memT[:, 0:4, m * P:m * P + P], bank(key).rearrange("p (k t) -> p k t", k=4))
            act.wait_ge(rstd_new, 4)
            split_and_square("mem", 16, memT, mh, lambda k: emptied(act, ("mx", 1, k // 4)), KD)
            rstd_rows("stat_mem", RB2[:, 0:MT], D)
            for m in range(2):
                copy_out(("mko", m), mko[:, m, :], bank(("mko", m)))
            emptied(act, ("mko", 1))
            act.dma_start(o["mem_k_prompt"][0, 0].rearrange("(t p) h e -> p t (h e)", p=P), mko[:, :, :]).then_inc(mk_out, 16)
            for m in range(2):
                copy_out(("mvt", m), MV[:, m, :], bank(("mvt", m)))
            emptied(act, ("mvt", 1))
            act.dma_start(o["mem_v_prompt"][0, 0].rearrange("(t p) h e -> p t (h e)", p=P), MV[:, :, :]).then_inc(mv_out, 16)

            def memory_exp(n):
                act.wait_ge(m_max, n + 1)
                if n >= 2:
                    full(act, ("mpt", n - 2))
                for hh in range(2):
                    c = 2 * (n % 4) + hh
                    ins = act.activation(Pm[n % 2][:, hh, :], bank(("ms", n))[:, hh * MT:hh * MT + MT], ACT.Exp,
                                         bias=small[:, c:c + 1], accum_out=small[:, 8 + c:9 + c])
                ins.then_inc(freed["s"], 1)

            memory_exp(0)
            memory_exp(1)
            for n, (q, hp) in enumerate(munits):
                if n >= 2:
                    full(act, ("mpo", n - 2))
                copy_out(("mpt", n), PTm[n % 2][:, :, :].rearrange("p m q -> p (m q)"), bank(("mpt", n)))
                if n + 2 < len(munits):
                    memory_exp(n + 2)
                full(act, ("mpo", n))
                act.activation(omh[:, 2 * hp:2 * hp + 2, q * P:q * P + P], bank(("mpo", n))[:, 0:2 * P].rearrange("p (h q) -> p h q", h=2),
                               ACT.Copy).then_inc(om_hi, 1)
            act.wait_ge(s_max, 1)
            act.activation(scr[0:32, :], bank("sct")[0:32, 0:MT], ACT.Exp, bias=small[0:32, 40:41],
                           accum_out=small[0:32, 41:42]).then_inc(freed["s"], 1)
            full(act, "spo")
            act.activation(omh[:, :, T:TT], bank("spo")[:, 0:32].rearrange("p (h b) -> p h b", b=NS), ACT.Copy).then_inc(om_hi, 1)
            act.wait_ge(mk_out, 16)
            split_and_square("ffn", 24, XT, BH, lambda k: emptied(act, ("mo", k)), KD)
            rstd_rows("stat_ffn", RB1[:, :], D)
            act.wait_ge(mv_out, 16)
            for f in range(NF):
                act.wait_ge(conv_new, f + 1)
                act.activation(cu[:, :], cu[:, :], ACT.Exp, scale=-1.0).then_inc(conv_exp, 1)
                act.wait_ge(act_new, f + 1)
                act.activation(acth[:, f % FSLOTS, :], ct[:, :], ACT.Copy).then_inc(act_hi, 1)
            for f in range(0, NF, 4):
                w = (min(f + 4, NF) - f) * P
                copy_out(("tail", f), cvs[0:10, f * P:f * P + w], bank(("tail", f))[0:10, 0:w])
            emptied(act, ("tail", NF - 2))
            act.dma_start(o["conv_prompt"][0, 0], cvs[0:2, :]).then_inc(tail_out, 16)
            act.dma_start(o["conv_sample"][0, :, 1], cvs[2:10, :]).then_inc(tail_out, 16)
            last = len(FPARTS) - 1
            split_and_square("final", 32, XT, XG, lambda k: emptied(act, ("down", last, k)), KD)
            full(act, "rtok")
            act.activation(small[:, 0:NT], bank("rtok")[:, 0:NT], ACT.Ln, bias=eps[:, 0:1], scale=1.0 / D)
            step(act.activation(small[0:NS, NT:NT + 1], bank("rtok")[0:NS, NT:NT + 1], ACT.Ln, bias=eps[0:NS, 0:1], scale=1.0 / D))
            step(act.activation(small[:, 0:NT], small[:, 0:NT], ACT.Exp, scale=-0.5))
            act.activation(small[0:NS, NT:NT + 1], small[0:NS, NT:NT + 1], ACT.Exp, scale=-0.5).then_inc(freed["s"], 1)
            emptied(act, "rtok")
            act.wait_ge(tail_out, 32)
            for n in range(NT + 1):
                w = P if n < NT else NS
                key = ("y", n, 0)
                full(act, key)
                if n >= 4:
                    act.wait_ge(y_out[n % 4], 16 * (n // 4))
                act.activation(yst[n % 4][0:w, 0:512], bank(key)[0:w, :], ACT.Copy, scale=small[0:w, n:n + 1]).then_inc(freed["s"], 1)

        @block.vector
        def _(ve):
            steps = [0]

            def step(ins):
                steps[0] += 1
                ins.then_inc(vstep, 1)
                ve.wait_ge(vstep, steps[0])

            def bc(ap, axis, n):
                shape = list(ap.shape)
                return ap.unsqueeze(axis).broadcast_to(shape[:axis] + [n] + shape[axis:])

            taken = [0]

            def take(ins):
                taken[0] += 1
                ins.then_inc(freed["v"], 1)

            def take_now(ins):
                take(ins)
                ve.wait_ge(freed["v"], taken[0])

            def turned_x(n):
                w = P if n < NT else NS
                key = ("x", n, 1)
                full(ve, key)
                take(ve.tensor_copy(XT[:, 4:8, n * P:n * P + w], bank(key)[:, 0:4 * w].rearrange("p (k t) -> p k t", k=4)))

            for n in range(4):
                turned_x(n)
            ve.wait_ge(consts_in, 16 * CONSTS)
            ve.tensor_copy(SB[0:GT, 0, :].rearrange("g (a b) -> g a b", b=8), bc(OTMP[0:GT, 0, 0:GP].bitcast(I32), 2, 8)).then_inc(pg_new, 1)
            full(ve, "cst")
            ve.tensor_copy(gains[:, 0:54], bank("cst")[:, 0:54])
            take_now(ve.tensor_copy(convc[:, :], bank("cst")[:, 54:142]))
            full(ve, "scv")
            take(ve.tensor_copy(sconv[:, :, :].rearrange("p f r -> p (f r)"), bank("scv")[:, 0:NF * 16]))
            full(ve, "idx")
            take(ve.tensor_scalar(idx[:, :], bank("idx")[:, 0:GT], 8.0, rowof[:, 0:1], ALU.mult, ALU.add))
            step(ve.tensor_tensor(lbt[:, 0:4], gains[:, 46:50], gains[:, 50:54], ALU.max))
            ve.tensor_tensor(lbt[:, 4:8], gains[:, 46:50], lbt[:, 0:4], ALU.subtract)
            ve.tensor_tensor(lbt[:, 8:12], gains[:, 50:54], lbt[:, 0:4], ALU.subtract).then_inc(lb_diff, 1)
            ve.wait_ge(lb_exp, 1)
            step(ve.tensor_tensor(lbt[:, 12:16], lbt[:, 4:8], lbt[:, 8:12], ALU.add))
            step(ve.reciprocal(lbt[:, 12:16], lbt[:, 12:16]))
            step(ve.tensor_tensor(lbt[:, 16:20], lbt[:, 4:8], lbt[:, 12:16], ALU.mult))
            step(ve.tensor_scalar(lbt[:, 20:24], lbt[:, 16:20], -1.0, 1.0, ALU.mult, ALU.add))
            for n in range(4, NT + 1):
                turned_x(n)

            split_no, added = [0], [0]

            def split_and_sum(gain, src, hi, lo, n, before=lambda k: None):
                w = src.shape[2]
                for k in range(n):
                    before(k)
                    split_no[0] += 1
                    ve.wait_ge(hi_done, split_no[0])
                    if lo is not None:
                        ve.scalar_tensor_tensor(out=lo[:, k, :], in0=src[:, k, :], scalar=gains[:, gain + k:gain + k + 1],
                                                in1=hi[:, k, :], op0=ALU.mult, op1=ALU.subtract).then_inc(lo_done, 1)
                    ve.wait_ge(sq_done, split_no[0])
                    if k:
                        if k > 1:
                            ve.wait_ge(ss_done, added[0])
                        added[0] += 1
                        ve.tensor_tensor(SS[:, 0:w], SS[:, 0:w], SQ[:, 0:w], ALU.add).then_inc(ss_done, 1)

            emptied(ve, ("x", NT, 0))
            split_and_sum(0, XT, XH, XL, KD)
            ve.wait_ge(ss_done, 7)
            full(ve, "stat_mix")
            step(ve.memset(RM[:, :], 1.0))
            step(ve.memset(RM[:, :].rearrange("p (c t) -> p c t", t=CK)[:, :, 0:1], 0.0))

            def refine(key, r, w=TT):
                emptied(ve, key)
                var, r = SS[:, 0:w], r[:, 0:w]
                step(ve.scalar_tensor_tensor(out=var, in0=var, scalar=-0.5, in1=r, op0=ALU.mult, op1=ALU.mult))
                step(ve.tensor_tensor(var, var, r, ALU.mult))
                ve.scalar_tensor_tensor(out=r, in0=var, scalar=1.5, in1=r, op0=ALU.add, op1=ALU.mult).then_inc(rstd_new, 1)
                refined[0] += 1
                ve.wait_ge(rstd_new, refined[0])

            refined = [0]

            def scaled(key, out, r):
                full(ve, key)
                take_now(ve.tensor_tensor(by3(out), chunks(key), by3(r), ALU.mult))

            def hg_forget(h):
                ve.wait_ge(f_exp, h + 1)
                step(ve.tensor_scalar(t0[:, :], t0[:, :], 1.0, None, ALU.add))
                step(ve.reciprocal(t0[:, :], t0[:, :]))
                ve.tensor_scalar(t0[:, :], t0[:, :], lbt[:, 20 + h:21 + h], lbt[:, 16 + h:17 + h], ALU.mult, ALU.add).then_inc(f_new, 1)

            def hg_gate(h):
                ve.wait_ge(g_exp, h + 1)
                step(ve.tensor_scalar(v0[:, :], v0[:, :], 1.0, None, ALU.add))
                step(ve.reciprocal(v0[:, :], v0[:, :]))
                ve.tensor_tensor(HGO[:, h, :], HGO[:, h, :], v0[:, :], ALU.mult).then_inc(gate_new, 1)
                ve.wait_ge(gate_new, h + 1)

            def hg_sums(h):
                ve.wait_ge(f_new, h + 1)
                step(ve.tensor_scalar(t1[:, :], t0[:, :], -1.0, 1.0, ALU.mult, ALU.add))
                ve.tensor_copy(rows_of(h)[:, 0:NS], t1[:, T:TT])
                step(ve.tensor_copy(rows_of(h)[:, NS:2 * NS], t0[:, T:TT]))
                ve.wait_ge(f_log, h + 1)
                for c in range(0, T, 256):
                    ins = ve.tensor_tensor_scan(t0[:, c:c + 256], RM[:, :], t2[:, c:c + 256], 0.0, ALU.mult, ALU.add)
                ins.then_inc(b_new, 1)

            def hg_keys(h):
                q = tq[h % 2]
                ve.wait_ge(b_exp, h + 1)
                ve.tensor_tensor(q[:, 0:T], q[:, 0:T], t2[:, 0:T], ALU.mult)
                step(ve.tensor_copy(dec[:, :], t2[:, 0:T].rearrange("p (c t) -> p c t", t=CK)[:, :, CK - 1]))
                ve.wait_ge(b_nexp, h + 1)
                step(ve.tensor_tensor(t1[:, 0:T], t1[:, 0:T], t0[:, 0:T], ALU.mult))
                ve.tensor_tensor(t2[:, 0:T].rearrange("p (c t) -> p c t", t=CK), t1[:, 0:T].rearrange("p (c t) -> p c t", t=CK),
                                 bc(dec[:, :], 2, CK), ALU.mult).then_inc(qk_new, 1)

            def hg_chain(h, half):
                if half:
                    full(ve, ("o", h, 0))
                    step(ve.tensor_copy(Sst[:, 0, :], Sst[:, 16, :]))
                else:
                    if h:
                        full(ve, ("o", h - 1, 1))
                        ve.wait_ge(hst_out, 16 * h)
                    step(ve.memset(Sst[:, 0, :], 0.0))
                for n in range(4):
                    key = ("u", h, half, n)
                    full(ve, key)
                    for c in range(4):
                        k = 4 * n + c
                        ins = ve.scalar_tensor_tensor(out=Sst[:, k + 1, :], in0=Sst[:, k, :], scalar=dec[:, 16 * half + k:16 * half + k + 1],
                                                      in1=bank(key)[:, c * P:c * P + P], op0=ALU.mult, op1=ALU.add)
                        take_now(ins) if c == 3 else step(ins)
                key = ("a", h, half)
                full(ve, key)
                if h or half:
                    full(ve, ("o", h, 0) if half else ("o", h - 1, 1))
                step(ve.memset(AT[:, :, :], 0.0))
                take_now(ve.copy_predicated(AT[:, :, :], bc(hmask[:, :], 1, 4), bank(key).rearrange("p (n t) -> p n t", n=4)))

            def hg_norm(h, half):
                e = 2 * h + half
                ve.wait_ge(o_sq, e + 1)
                ve.tensor_reduce(smp[:, 16:20], ON[:, :, :], AX, ALU.add).then_inc(o_ms, 1)
                ve.wait_ge(o_rstd, e + 1)
                take_now(ve.tensor_tensor(ON[:, :, :], bank(("o", h, half)).rearrange("p (n v) -> p n v", n=4),
                                          bc(smp[:, 20:24], 2, P), ALU.mult))
                key = ("ot", h, half)
                full(ve, key)
                g = HGO[:, h, 512 * half:512 * half + 512]
                take_now(ve.scalar_tensor_tensor(out=g, in0=bank(key), scalar=gains[:, 45:46], in1=g, op0=ALU.mult, op1=ALU.mult))

            def hg_sample_rows(h):
                key = ("ts", h)
                full(ve, key)
                ve.tensor_copy(small[0:NS, :], bank(key)[0:NS, 0:P])
                take_now(ve.tensor_tensor(OTMP[0:NS, :, :], bc(bank(key)[0:NS, P:2 * P], 1, NS), bc(ident[0:NS, 0:NS], 2, P), ALU.mult))

            def hg_sample_states(h):
                key = ("sk", h)
                ve.wait_ge(sb_in, 16 * (h + 1))
                full(ve, key)
                for b in range(NS):
                    ins = ve.scalar_tensor_tensor(out=SB[:, b, :], in0=SB[:, b, :], scalar=rows_of(h)[:, NS + b:NS + b + 1],
                                                  in1=bank(key, b // 4)[:, (b % 4) * P:(b % 4 + 1) * P], op0=ALU.mult, op1=ALU.add)
                take_now(ins)
                key = ("so", h)
                full(ve, key)
                b0 = uses[key][1][0]
                take_now(ve.tensor_tensor(OTMP[32:32 + NS, :, :], PS[0:NS, b0:b0 + 2, :].rearrange("p n (b v) -> p (n b) v", b=4),
                                          bc(ident[0:NS, 0:NS], 2, P), ALU.mult))
                step(ve.tensor_reduce(OTMP[0:NS, 0, :], OTMP[32:32 + NS, :, :].rearrange("p b v -> p v b"), AX, ALU.add))
                step(ve.tensor_tensor(OTMP[0:NS, 1, :], OTMP[0:NS, 0, :], OTMP[0:NS, 0, :], ALU.mult))
                ve.tensor_reduce(OTMP[0:NS, 2, 0:1], OTMP[0:NS, 1, :], AX, ALU.add).then_inc(os_ms, 1)
                ve.wait_ge(os_rstd, h + 1)
                ve.tensor_scalar(OTMP[0:NS, 0, :], OTMP[0:NS, 0, :], OTMP[0:NS, 2, 1:2], None, ALU.mult).then_inc(os_new, 1)
                key = ("sot", h)
                full(ve, key)
                g = HGO[:, h, T:TT]
                take_now(ve.scalar_tensor_tensor(out=g, in0=bank(key)[:, 0:NS], scalar=gains[:, 45:46], in1=g, op0=ALU.mult, op1=ALU.mult))

            refine("stat_mix", RB1)
            for h in range(HG):
                scaled(("f", h), t0[:, :], RB1[:, :])
                ve.tensor_scalar(t0[:, :], t0[:, :], XMIN, None, ALU.max).then_inc(f_raw, 1)
                if h:
                    hg_sample_rows(h - 1)
                scaled(("g", h), HGO[:, h, :], RB1[:, :])
                ve.tensor_scalar(v0[:, :], HGO[:, h, :], XMIN, None, ALU.max).then_inc(g_raw, 1)
                if h:
                    hg_chain(h - 1, 0)
                hg_forget(h)
                scaled(("q", h), tq[h % 2][:, :], RB1[:, :])
                if h:
                    hg_norm(h - 1, 0)
                    hg_chain(h - 1, 1)
                hg_sums(h)
                hg_gate(h)
                scaled(("i", h), v0[:, :], RB1[:, :])
                if h:
                    hg_norm(h - 1, 1)
                    hg_sample_states(h - 1)
                hg_keys(h)
            hg_sample_rows(HG - 1)
            hg_chain(HG - 1, 0)
            hg_norm(HG - 1, 0)
            hg_chain(HG - 1, 1)
            hg_norm(HG - 1, 1)
            hg_sample_states(HG - 1)

            for c in range(KV):
                scaled(("ckv", c), ckvT[:, c, :], RB1[:, :])
            ve.wait_ge(kv_sq, 2)
            ve.tensor_tensor(SS[:, :], SS[:, :], SQ[:, :], ALU.add).then_inc(kv_sum, 1)
            ve.wait_ge(kv_sum, 1)
            full(ve, "kr")
            ve.wait_ge(trig_in, 16)
            ve.tensor_tensor(by3(trig[96:P, :]), chunks("kr", 64, 96), by3(trig[0:32, :]), ALU.mult)
            take_now(ve.tensor_tensor(by3(SQ[96:P, :]), chunks("kr", 96, P), by3(trig[32:64, :]), ALU.mult))
            step(ve.tensor_tensor(trig[96:P, :], trig[96:P, :], SQ[96:P, :], ALU.add))
            ve.tensor_tensor(trig[96:P, :], trig[96:P, :], RB1[96:P, :], ALU.mult).then_inc(krT_new, 1)
            refine("stat_kv", RB2)
            for c in range(KV):
                ve.scalar_tensor_tensor(out=ckvT[:, c, :], in0=ckvT[:, c, :], scalar=gains[:, 43 + c:44 + c], in1=RB2[:, :],
                                        op0=ALU.mult, op1=ALU.mult).then_inc(kv_new, 1)
            for c in range(KQ):
                scaled(("cq", c), cqr[:, c, :], RB1[:, :])
            split_and_sum(40, cqr, cqh, cql, KQ)
            refine("stat_q", RB1)
            step(ve.scalar_tensor_tensor(out=trig[0:64, :], in0=trig[0:64, :], scalar=SCALE, in1=RB1[0:64, :], op0=ALU.mult, op1=ALU.mult))
            for h in range(H):
                key = ("uq", h)
                full(ve, key)
                ve.scalar_tensor_tensor(out=by3(qT[0:64, h, :]), in0=chunks(key, 0, 64), scalar=SCALE, in1=by3(RB1[0:64, :]),
                                        op0=ALU.mult, op1=ALU.mult)
                ve.tensor_tensor(by3(qT[64:96, h, :]), chunks(key, 64, 96), by3(trig[0:32, :]), ALU.mult)
                take_now(ve.tensor_tensor(by3(SQ[64:96, :]), chunks(key, 96, P), by3(trig[32:64, :]), ALU.mult))
                ve.tensor_tensor(qT[64:96, h, :], qT[64:96, h, :], SQ[64:96, :], ALU.add).then_inc(q_new, 1)
                ve.wait_ge(q_new, h + 1)
            for c in range(KV):
                ve.wait_ge(kv_hi, c + 1)
                ve.tensor_tensor(ckl[:, c, :], ckvT[:, c, :], ckh[:, c, :], ALU.subtract).then_inc(kv_lo, 1)
            for n in range(0, NT, 2):
                key = ("ckvo", n)
                full(ve, key)
                take(ve.tensor_copy(ckvo[:, n:n + 2, :].rearrange("p n l -> p (n l)"), bank(key)))
            full(ve, "ckvs")
            take_now(ve.tensor_copy(ckvo[0:NS, NT, :], bank("ckvs")[0:NS, 0:KVL]))
            ve.tensor_copy(small[:, 0:16].rearrange("p (c b) -> p c b", c=KV), ckvT[:, :, T:TT])
            ve.tensor_copy(small[96:P, 16:24], trig[96:P, T:TT])
            step(ve.tensor_copy(small[0:QK, 24:88].rearrange("p (h b) -> p h b", h=H), qT[0:QK, :, T:TT]))

            def softmax_max(n, u):
                q, h = u
                w = (q + 1) * P
                key = ("S", u)
                full(ve, key)
                b0 = uses[key][1][0]
                diagonal = PS[:, b0 + q // 4, (q % 4) * P:(q % 4 + 1) * P]
                step(ve.tensor_tensor(diagonal, diagonal, causal[:, :], ALU.add))
                ve.tensor_reduce(small[:, 96 + n % 4:97 + n % 4], PS[:, b0:b0 + 2, :].rearrange("p b k -> p (b k)")[:, 0:w], AX, ALU.max,
                                 negate=True).then_inc(p_max, 1)

            def softmax_scale(n, u):
                w = (u[0] + 1) * P
                emptied(ve, ("S", u))
                step(ve.reciprocal(small[:, 104 + n % 4:105 + n % 4], small[:, 100 + n % 4:101 + n % 4]))
                ve.tensor_scalar(Pr[n % 2][:, 0:w], Pr[n % 2][:, 0:w], small[:, 104 + n % 4:105 + n % 4], None, ALU.mult).then_inc(p_new, 1)

            softmax_max(0, units[0])
            softmax_max(1, units[1])
            softmax_scale(0, units[0])
            for n, u in enumerate(units):
                q, h = u
                if q >= 4:
                    key = ("pt", u, 1)
                    full(ve, key)
                    if n >= 2:
                        full(ve, ("po", units[n - 2][0], units[n - 2][1] // 2)) if units[n - 2][1] % 2 else ve.wait_ge(even_done, (n - 2) // 2 + 1)
                    take(ve.tensor_copy(PTr[n % 2][:, 4:q + 1, :].rearrange("p m q -> p (m q)"), bank(key)[:, 0:(q - 3) * P]))
                if n + 1 < len(units):
                    softmax_scale(n + 1, units[n + 1])
                if n + 2 < len(units):
                    softmax_max(n + 2, units[n + 2])

            full(ve, ("po", NT - 1, H // 2 - 1))
            step(ve.memset(qrz[:, :, :, :], 0.0))
            for n in range(4):
                ins = ve.tensor_copy(qrz[32 * n:32 * n + 32, :, n, 0:H], small[64:96, 24:88].rearrange("p (h b) -> p b h", h=H))
            ve.memset(qlat[:, :, :, :], 0.0).then_inc(lat_zero, 1)
            ve.tensor_copy(krs0, small[96:P, 16:24]).then_inc(qz_new, 1)
            for n in (1, 3):
                full(ve, ("wk", n))
                take(ve.tensor_copy(wukT[0:NOPE, 2 * n:2 * n + 2, :].rearrange("p h l -> p (h l)"), bank(("wk", n))[0:NOPE, :]))
            full(ve, "qlat")
            ve.wait_ge(lat_zero, 1)
            take(ve.tensor_copy(qlat[:, :, :, 0:H], bank("qlat")[:, 0:P].rearrange("p (c h b) -> p c b h", c=KV, h=H)))

            def keys_out(g, first, last):
                for j in range(first, last):
                    key = ("kt", g, j, 1)
                    full(ve, key)
                    take(ve.tensor_copy(KT[:, j, 1, :], bank(key)))

            def sequence_sum(b):
                ve.tensor_reduce(nmS[:, b:b + 1], nmax[:, NG * b:NG * b + NG], AX, ALU.min).then_inc(seq_w, 1)
                ve.wait_ge(seq_wd, b + 1)
                step(ve.tensor_tensor(lprod, lsum[:, NG * b:NG * b + NG], wgt, ALU.mult))
                ve.tensor_reduce(Lseq[:, b:b + 1], lprod, AX, ALU.add)
                emptied(ve, ("go", NG * b + NG - 1))
                step(ve.tensor_scalar(Oacc[:, b, :], Og[:, 0, :], wgt[:, 0:1], None, ALU.mult))
                for n in range(1, NG):
                    ins = ve.scalar_tensor_tensor(out=Oacc[:, b, :], in0=Og[:, n, :], scalar=wgt[:, n:n + 1], in1=Oacc[:, b, :],
                                                  op0=ALU.mult, op1=ALU.add)
                    if n + 1 < NG:
                        step(ins)
                ins.then_inc(seq_o, 1)

            keys_out(0, 0, 4)
            for g in range(GT):
                key = ("gs", g)
                full(ve, key)
                ve.tensor_reduce(nmax[:, g:g + 1], bank(key), AX, ALU.max, negate=True).then_inc(g_max, 1)
                if g and g % NG == 0:
                    ve.wait_ge(g_max, g)
                    sequence_sum(g // NG - 1)
                if g + 1 < GT:
                    keys_out(g + 1, 0, 3)
                key = ("gpt", g)
                full(ve, key)
                if g:
                    full(ve, ("go", g - 1))
                take(ve.tensor_copy(PTs[:, :, :].rearrange("p n k -> p (n k)"), bank(key)))
                if g + 1 < GT:
                    keys_out(g + 1, 3, 4)
            ve.wait_ge(g_max, GT)
            sequence_sum(NS - 1)
            full(ve, "m1")
            step(ve.tensor_reduce(nMx, bank("m1")[0:NS, 0:P].rearrange("p (j h) -> p h j", j=4), AX, ALU.min))
            take(ve.tensor_copy(expd[:, 0:1], nMx[:, 0:1]))
            full(ve, "snew")
            take_now(ve.tensor_tensor(sprod, bank("snew")[0:NS, 0:256].rearrange("p (b h) -> p b h", b=NS), bc(ident[0:NS, 0:NS], 2, 32), ALU.mult))
            step(ve.tensor_reduce(snew, sprod.rearrange("p b h -> p h b"), AX, ALU.add))
            step(ve.scalar_tensor_tensor(out=nMx, in0=snew, scalar=-1.0, in1=nMx, op0=ALU.mult, op1=ALU.min))
            ve.tensor_tensor(wnew, snew, nMx, ALU.add).then_inc(c_new, 1)
            ve.tensor_copy(expd.rearrange("p (j h) -> p j h", j=4), bc(nMx, 1, 4)).then_inc(c_diff, 1)
            full(ve, "m2")
            take_now(ve.tensor_tensor(fac, bank("m2")[:, 0:NS], nmS, ALU.subtract))
            ve.tensor_copy(lprod[:, 0:1], fac[:, 0:1]).then_inc(c_diff, 1)
            ve.wait_ge(c_fac, 1)
            ve.wait_ge(c_exp, 1)
            step(ve.tensor_tensor(Oacc[:, :, :], Oacc[:, :, :], bc(fac, 2, KVL), ALU.mult))
            step(ve.tensor_tensor(Lseq, Lseq, fac, ALU.mult))
            ve.tensor_tensor(WD.rearrange("p (b h) -> p b h", b=NS), bc(wnew[:, 0:H], 1, NS), bc(ident[0:NS, 0:NS], 2, H), ALU.mult)
            ve.tensor_tensor(LS.rearrange("p (b h) -> p b h", b=NS), bc(Lseq, 2, H), bc(sel[:, :], 1, NS), ALU.mult).then_inc(ls_new, 1)
            full(ve, "fin")
            fin = bank("fin")
            for c in range(KV):
                ins = ve.tensor_tensor(ltmp[:, c, :, :], fin[:, 64:P].rearrange("p (b h) -> p b h", b=NS), bc(small[:, 8 * c:8 * c + 8], 2, H), ALU.mult)
            step(ins)
            ve.tensor_tensor(lat.rearrange("p c b h -> p (c b h)"), fin[:, P:2 * P], ltmp.rearrange("p c b h -> p (c b h)"), ALU.add)
            take_now(ve.reciprocal(LS, fin[:, 0:64]))
            for c in range(KV):
                ins = ve.tensor_tensor(lat[:, c, :, :], lat[:, c, :, :], LS.rearrange("p (b h) -> p b h", b=NS), ALU.mult)
            ins.then_inc(lat_new, 1)
            full(ve, "oT")
            oT = bank("oT")[:, 0:64].rearrange("p (q b e) -> p e q b", q=4, b=NS)
            ve.tensor_copy(MO[0:64, :, T:TT], oT[0:64, 0, :, :])
            take(ve.tensor_copy(MO[64:P, :, T:TT], oT[64:P, 1, :, :]))

            for n in range(KD):
                t = (n + 4) % KD
                src = MO[:, t, :] if t < 4 else HGO[:, t - 4, :]
                ve.wait_ge(cat_hi, n + 1)
                ve.tensor_tensor(CLo[:, t, :], src, CHi[:, t, :], ALU.subtract).then_inc(cat_lo, 1)

            def residual(name):
                def add(k):
                    key = (*name, k)
                    full(ve, key)
                    take_now(ve.tensor_tensor(by3(XT[:, k, :]), chunks(key), by3(XT[:, k, :]), ALU.add))
                return add

            split_and_sum(8, XT, BH, BL, KD, residual(("out",)))
            refine("stat_memx", RB1)

            def queries_out(h):
                key = ("mq", h)
                full(ve, key)
                take(ve.scalar_tensor_tensor(out=by3(qm[:, h, :]), in0=chunks(key), scalar=MSCALE, in1=by3(RB1[:, :]), op0=ALU.mult, op1=ALU.mult))

            queries_out(0)
            for m in range(2):
                key = ("mx", m, 1)
                full(ve, key)
                take(ve.tensor_copy(memT[:, 4:8, m * P:m * P + P], bank(key).rearrange("p (k t) -> p k t", k=4)))
            split_and_sum(16, memT, mh, ml, KD, lambda k: emptied(ve, ("mx", 1, k // 4)))
            for h in range(1, MH):
                queries_out(h)
            refine("stat_mem", RB2, MT)
            for name, dst in (("mk", MKT), ("mv", mvT)):
                for h in range(MH):
                    key = (name, h)
                    full(ve, key)
                    take(ve.tensor_tensor(dst[:, h, :], bank(key)[:, 0:MT], RB2[:, 0:MT], ALU.mult))
            full(ve, "qs")
            take_now(ve.tensor_copy(QS[0:NS, :], bank("qs")[0:NS, :]))
            ve.tensor_copy(OH[0:NS, :, :], bc(ident[0:NS, 0:NS], 2, P)).then_inc(qs_set, 1)

            def memory_max(n):
                full(ve, ("ms", n))
                c = 2 * (n % 4)
                ve.tensor_reduce(small[:, c:c + 2], bank(("ms", n)).rearrange("p (h m) -> p h m", h=2), AX, ALU.max, negate=True).then_inc(m_max, 1)

            memory_max(0)
            memory_max(1)

            def memory_scale(n):
                c = 2 * (n % 4)
                emptied(ve, ("ms", n))
                step(ve.reciprocal(small[:, 16 + c:18 + c], small[:, 8 + c:10 + c]))
                ve.tensor_tensor(Pm[n % 2][:, :, :], Pm[n % 2][:, :, :], bc(small[:, 16 + c:18 + c], 2, MT), ALU.mult).then_inc(m_new, 1)

            memory_scale(0)
            for n, (q, hp) in enumerate(munits):
                if n + 1 < len(munits):
                    memory_scale(n + 1)
                if n + 2 < len(munits):
                    memory_max(n + 2)
                ve.wait_ge(om_hi, n + 1)
                take(ve.tensor_tensor(oml[:, 2 * hp:2 * hp + 2, q * P:q * P + P], bank(("mpo", n))[:, 0:2 * P].rearrange("p (h q) -> p h q", h=2),
                                      omh[:, 2 * hp:2 * hp + 2, q * P:q * P + P], ALU.subtract))
                if n % 2 == 0:
                    b = n // 2
                    full(ve, ("qb", b))
                    ve.wait_ge(sk_in[b % 2], 16 * (b // 2 + 1))
                    take_now(ve.tensor_tensor(prod[:, :, :], sK[b % 2][:, :, :], bc(bank(("qb", b)), 1, 2), ALU.mult))
                    ve.tensor_reduce(sc[:, :, MH * b:MH * b + MH], prod[:, :, :].rearrange("p t (h e) -> p t h e", h=MH), AX, ALU.add).then_inc(prod_done, 1)
                    ve.wait_ge(prod_done, b + 1)
            full(ve, "sct")
            ve.tensor_reduce(small[0:32, 40:41], bank("sct")[0:32, 0:MT], AX, ALU.max, negate=True).then_inc(s_max, 1)
            emptied(ve, "sct")
            step(ve.reciprocal(small[0:32, 42:43], small[0:32, 41:42]))
            ve.tensor_scalar(scr[0:32, :], scr[0:32, :], small[0:32, 42:43], None, ALU.mult).then_inc(s_new2, 1)
            full(ve, "spt")
            take(ve.tensor_copy(pm[:, :, :].rearrange("p m n -> p (m n)"), bank("spt")[:, 0:64]))
            full(ve, "spv")
            take(ve.tensor_copy(prod[:, :, :], PS[:, uses["spv"][1][0]:uses["spv"][1][0] + 2, :]))
            ve.wait_ge(om_hi, len(munits) + 1)
            take(ve.tensor_tensor(oml[:, :, T:TT], bank("spo")[:, 0:32].rearrange("p (h b) -> p h b", b=NS), omh[:, :, T:TT], ALU.subtract))
            split_and_sum(24, XT, BH, BL, KD, residual(("mo",)))

            refine("stat_ffn", RB1)
            step(ve.memset(ab[:, 0:2], 0.0))

            def tap(out, in0, f, t, **kw):
                return ve.scalar_tensor_tensor(out=out, in0=in0, scalar=convc[:, t * NF + f:t * NF + f + 1], in1=out, op0=ALU.mult, op1=ALU.add)

            def ffn_tile(f):
                scaled(("a", f), ab[:, 2:TT + 2], RB1[:, :])
                ve.tensor_copy(atail[:, f, :], ab[:, T:TT + 2])
                step(ve.tensor_scalar(ct[:, :], ab[:, 2:TT + 2], convc[:, 2 * NF + f:2 * NF + f + 1], convc[:, 3 * NF + f:3 * NF + f + 1], ALU.mult, ALU.add))
                step(tap(ct[:, 0:T], ab[:, 1:T + 1], f, 1))
                tap(ct[:, 0:T], ab[:, 0:T], f, 0)
                rows = sconv[:, f, :].rearrange("p (b r) -> p r b", r=2)
                step(tap(ct[:, T:TT], rows[:, 1, :], f, 1))
                step(tap(ct[:, T:TT], rows[:, 0, :], f, 0))
                ve.tensor_scalar(cu[:, :], ct[:, :], XMIN, None, ALU.max).then_inc(conv_new, 1)
                ve.wait_ge(conv_exp, f + 1)
                step(ve.tensor_scalar(cu[:, :], cu[:, :], 1.0, None, ALU.add))
                step(ve.reciprocal(cu[:, :], cu[:, :]))
                step(ve.tensor_tensor(ct[:, :], ct[:, :], cu[:, :], ALU.mult))
                scaled(("b", f), cu[:, :], RB1[:, :])
                ve.tensor_tensor(ct[:, :], ct[:, :], cu[:, :], ALU.mult).then_inc(act_new, 1)
                ve.wait_ge(act_hi, f + 1)
                ve.tensor_tensor(actl[:, f % FSLOTS, :], ct[:, :], acth[:, f % FSLOTS, :], ALU.subtract).then_inc(act_lo, 1)
                ve.wait_ge(act_lo, f + 1)

            last = len(FPARTS) - 1
            for kind, what in ffn_order():
                if kind == "up":
                    ffn_tile(what)
                elif what[0] < last:
                    residual(("down", what[0]))(what[1])
            split_and_sum(32, XT, XG, None, KD, residual(("down", last)))
            emptied(ve, "rtok")
            for n in range(NT + 1):
                w = P if n < NT else NS
                key = ("y", n, 1)
                full(ve, key)
                if n == 0:
                    ve.wait_ge(tail_out, 32)
                if n >= 4:
                    ve.wait_ge(y_out[n % 4], 16 * (n // 4))
                take(ve.tensor_scalar(yst[n % 4][0:w, 512:D], bank(key)[0:w, :], small[0:w, n:n + 1], None, ALU.mult))


_INS = ['x_prompt', 'x_sample', 'mem_prompt', 'cache_ckv', 'cache_krope', 'page_table', 'cache_mem_k', 'cache_mem_v',
        'state_hgrn', 'state_conv', 'norm_mix', 'w_in', 'norm_q', 'norm_kv', 'w_uq', 'w_uk', 'w_uv', 'hg_lb_raw', 'norm_hg',
        'w_out', 'norm_memx', 'norm_mem', 'w_mq', 'w_mk', 'w_mv', 'w_mo', 'norm_ffn', 'w_up', 'conv_w', 'conv_b', 'w_down',
        'norm_final']
_OUTS = [("y_prompt", (1, T, D)), ("y_sample", (NS, 1, D)), ("ckv_prompt", (1, 1, T, KVL)), ("krope_prompt", (1, 1, T, ROPE)),
         ("mem_k_prompt", (1, 1, MT, MH, P)), ("mem_v_prompt", (1, 1, MT, MH, P)), ("hgrn_prompt", (1, 1, HG, DK, P)),
         ("conv_prompt", (1, 1, 2, FF)), ("ckv_sample", (1, NS, 1, KVL)), ("krope_sample", (1, NS, 1, ROPE)),
         ("hgrn_sample", (1, NS, HG, DK, P)), ("conv_sample", (1, NS, 2, FF))]


def _constants():
    r, c = np.arange(P)[:, None], np.arange(P)[None, :]
    half = ROPE // 2
    inv = np.float32(10000.0) ** (-np.arange(half, dtype=np.float32) / np.float32(half))
    pos = np.concatenate([np.arange(T), np.full(NS, NPG * PAGE)]).astype(np.float32)
    ang = inv.astype(np.float32)[:, None] * pos[None, :]
    cos, sin = np.cos(ang).astype(np.float32), np.sin(ang).astype(np.float32)
    half_, h, b4 = (a.reshape(1, -1) for a in np.meshgrid(range(2), range(MH), range(4), indexing="ij"))
    return {
        "selv": (r == 32 * b4 + MH * (4 * half_ + b4) + h).astype(np.float32),
        "ident": np.eye(P, dtype=np.float32),
        "causal": np.where(c > r, NEG, 0.0).astype(np.float32),
        "hmask": ((r // CK == c // CK) & (r <= c)).astype(np.uint32),
        "sel": ((r % 32) == np.arange(8)[None, :]).astype(np.float32),
        "rowof": (r % 8).astype(np.float32),
        "trig": np.concatenate([cos, cos, -sin, sin]),
    }


def kernel(**inputs):
    import concourse.bacc as _bacc
    from concourse.bass_utils import run_bass_kernel_spmd as _run

    nc = _bacc.Bacc("TRN2", target_bir_lowering=False, num_devices=1)
    arrays = {n: np.ascontiguousarray(inputs[n]) for n in _INS} | _constants()
    ins, outs = {}, {}
    for name, a in arrays.items():
        ins[name] = nc.dram_tensor(f"in_{name}_dram", a.shape, mybir.dt.from_np(a.dtype), kind="ExternalInput").ap()
    for name, shape in _OUTS:
        outs[name] = nc.dram_tensor(f"out_{name}_dram", shape, F32, kind="ExternalOutput").ap()
    build_program(nc, ins, outs)
    r = _run(nc, [{f"in_{n}_dram": a for n, a in arrays.items()}], core_ids=[0])
    return tuple(r.results[0][f"out_{name}_dram"] for name, _ in _OUTS)
```
